# Optimizing a Trainium2 kernel written in Bass

```python
import math
import jax
import jax.numpy as jnp
from jax import lax
import numpy as np

D_MODEL = 1024
BATCH = 1
SEQ = 1024
DEPTH = 1

W_A = 256
A_GROUPS = 4
CHUNK = 128
W_B = 256
CONV_WIDTH = 3
DILATION_PATTERNS = ((128, 1), (512, 4), (2048, 16))
C_GROUPS = 3
C_HEADS_PER_GROUP = 4
C_HEADS = C_GROUPS * C_HEADS_PER_GROUP
C_HEAD_DIM = 64
W_C_QKV = C_HEADS * C_HEAD_DIM
W_C = C_HEADS_PER_GROUP * C_HEAD_DIM
POOL_WINDOWS = (2, 4, 8, 16)
POOL_GROUPS = 4
W_D = 256
D_GROUP = W_D // POOL_GROUPS
N_BRANCH = 4
D_FF = 4 * D_MODEL
N_BUCKETS = 32
MAX_DISTANCE = 2048
EPS = 1e-6

IN_SPLITS = (W_A, W_A, W_B, W_B, W_B, W_C_QKV, W_C_QKV, W_C_QKV, W_D, N_BRANCH * D_MODEL)
D_IN = sum(IN_SPLITS)

kernel_name = "hybrid_gated_parallel_mixers"

def rmsnorm(x, g):
    x32 = x.astype(jnp.float32)
    y = x32 * lax.rsqrt(jnp.mean(jnp.square(x32), axis=-1, keepdims=True) + EPS)
    return y.astype(x.dtype) * g

def layernorm(x, g, b):
    x32 = x.astype(jnp.float32)
    mu = jnp.mean(x32, axis=-1, keepdims=True)
    var = jnp.mean(jnp.square(x32 - mu), axis=-1, keepdims=True)
    return ((x32 - mu) * lax.rsqrt(var + EPS)).astype(x.dtype) * g + b

def gmlp_spatial_gate(u, v, ln_g, ln_b, w_s, b_s):
    B, S, _ = v.shape
    u = jax.nn.gelu(u)
    v = layernorm(jax.nn.gelu(v), ln_g, ln_b)
    vc = v.reshape(B, S // CHUNK, CHUNK, A_GROUPS, W_A // A_GROUPS)
    causal = jnp.tril(jnp.ones((CHUNK, CHUNK), dtype=bool))
    w = jnp.where(causal[None], w_s, jnp.zeros_like(w_s))
    sv = jnp.einsum('gts,bcsgd->bctgd', w, vc) + b_s.T[None, None, :, :, None]
    return u * sv.reshape(B, S, W_A)

def causal_short_conv(z, w):
    S = z.shape[1]
    zp = jnp.pad(z, ((0, 0), (CONV_WIDTH - 1, 0), (0, 0)))
    y = w[0] * zp[:, 0:S]
    for j in range(1, CONV_WIDTH):
        y = y + w[j] * zp[:, j:j + S]
    return y

def t5_causal_bucket(dist):
    max_exact = N_BUCKETS // 2
    d_f = jnp.maximum(dist, 1).astype(jnp.float32)
    large = max_exact + (jnp.log(d_f / max_exact) / math.log(MAX_DISTANCE / max_exact)
                         * (N_BUCKETS - max_exact)).astype(jnp.int32)
    large = jnp.minimum(large, N_BUCKETS - 1)
    return jnp.where(dist < max_exact, dist, large)

def dilated_window_attention(q, k, v, bias_table, window, dil):
    B, S, H, Dh = q.shape
    n = window // dil
    Sp = -(-S // window) * window
    M = Sp // dil
    nb = M // n
    pad = ((0, 0), (0, Sp - S), (0, 0), (0, 0))

    def to_blocks(t):
        return jnp.pad(t, pad).reshape(B, nb, n, dil, H, Dh)

    def with_prev(t):
        prev = jnp.pad(t, ((0, 0), (1, 0), (0, 0), (0, 0), (0, 0), (0, 0)))[:, :nb]
        return jnp.concatenate([prev, t], axis=2)

    qb = to_blocks(q)
    kw = with_prev(to_blocks(k))
    vw = with_prev(to_blocks(v))
    s = jnp.einsum('bnqrhd,bnkrhd->bnrhqk', qb, kw).astype(jnp.float32) * (Dh ** -0.5)

    qi = jnp.arange(n)[:, None]
    ki = jnp.arange(2 * n)[None, :]
    delta = qi + n - ki
    band = (delta >= 0) & (delta <= n)
    blk = jnp.arange(nb)[:, None, None]
    valid = band[None] & ((blk > 0) | (ki >= n)[None])
    bias = bias_table[t5_causal_bucket(jnp.clip(delta, 0, None) * dil)]
    s = s + jnp.transpose(bias, (2, 0, 1)).astype(jnp.float32)[None, None, None]
    s = jnp.where(valid[None, :, None, None], s, -jnp.inf)
    m = jnp.max(s, axis=-1, keepdims=True)
    e = jnp.exp(s - m)
    den = jnp.sum(e, axis=-1, keepdims=True)
    o = jnp.einsum('bnrhqk,bnkrhd->bnqrhd', (e / den).astype(v.dtype), vw)
    lse = (m + jnp.log(den))[..., 0]
    o = o.reshape(B, Sp, H, Dh)[:, :S]
    lse = jnp.transpose(lse, (0, 1, 4, 2, 3)).reshape(B, Sp, H)[:, :S]
    return o, lse

def dilated_mixture(q, k, v, rel_bias):
    B, S, _ = q.shape
    shp = (B, S, C_GROUPS, C_HEADS_PER_GROUP, C_HEAD_DIM)
    q, k, v = q.reshape(shp), k.reshape(shp), v.reshape(shp)
    outs, lses = [], []
    for g, (window, dil) in enumerate(DILATION_PATTERNS):
        hs = slice(g * C_HEADS_PER_GROUP, (g + 1) * C_HEADS_PER_GROUP)
        o, lse = dilated_window_attention(q[:, :, g], k[:, :, g], v[:, :, g],
                                          rel_bias[:, hs], window, dil)
        outs.append(o)
        lses.append(lse)
    o = jnp.stack(outs, axis=2)
    alpha = jax.nn.softmax(jnp.stack(lses, axis=2), axis=2)
    out = jnp.einsum('bsgh,bsghd->bshd', alpha.astype(o.dtype), o)
    return out.reshape(B, S, W_C)

def multiscale_pool(z, w_pool, scale):
    B, S, _ = z.shape
    zg = z.reshape(B, S, POOL_GROUPS, D_GROUP).astype(jnp.float32)
    t = jnp.arange(S, dtype=jnp.float32)
    outs = []
    for gi, w in enumerate(POOL_WINDOWS):
        c = jnp.cumsum(zg[:, :, gi], axis=1)
        c_lag = jnp.pad(c, ((0, 0), (w, 0), (0, 0)))[:, :S]
        cnt = jnp.minimum(t + 1.0, float(w))
        outs.append((c - c_lag) / cnt[None, :, None])
    pooled = jnp.stack(outs, axis=2)
    y = (pooled - zg).astype(z.dtype)
    y = jnp.einsum('bsgd,gde->bsge', y, w_pool).reshape(B, S, W_D)
    return y * scale

def setup_inputs(seed: int = 0) -> dict:
    key = jax.random.key(seed)
    ks = jax.random.split(key, 21)
    L = DEPTH

    def nrm(k, shape, scale):
        return jax.random.normal(k, shape, jnp.float32) * scale

    return {
        "x": nrm(ks[0], (BATCH, SEQ, D_MODEL), 1.0),
        "norm_mix_g": 1.0 + nrm(ks[1], (L, D_MODEL), 0.05),
        "w_in": nrm(ks[2], (L, D_MODEL, D_IN), D_MODEL ** -0.5),
        "a_ln_g": 1.0 + nrm(ks[3], (L, W_A), 0.05),
        "a_ln_b": nrm(ks[4], (L, W_A), 0.02),
        "a_ws": nrm(ks[5], (L, A_GROUPS, CHUNK, CHUNK), CHUNK ** -0.5),
        "a_bs": 1.0 + nrm(ks[6], (L, A_GROUPS, CHUNK), 0.1),
        "w_a_out": nrm(ks[7], (L, W_A, D_MODEL), W_A ** -0.5),
        "b_conv": nrm(ks[8], (L, CONV_WIDTH, W_B), CONV_WIDTH ** -0.5),
        "w_b_out": nrm(ks[9], (L, W_B, D_MODEL), W_B ** -0.5),
        "rel_bias": nrm(ks[10], (N_BUCKETS, C_HEADS), 0.5),
        "w_c_out": nrm(ks[11], (L, W_C, D_MODEL), W_C ** -0.5),
        "d_w": nrm(ks[12], (L, POOL_GROUPS, D_GROUP, D_GROUP), D_GROUP ** -0.5),
        "d_scale": 1.0 + nrm(ks[13], (L, W_D), 0.1),
        "w_d_out": nrm(ks[14], (L, W_D, D_MODEL), W_D ** -0.5),
        "w_o": nrm(ks[15], (L, D_MODEL, D_MODEL), D_MODEL ** -0.5),
        "norm_ff_g": 1.0 + nrm(ks[16], (L, D_MODEL), 0.05),
        "w_ff1": nrm(ks[17], (L, D_MODEL, D_FF), D_MODEL ** -0.5),
        "w_ff2": nrm(ks[18], (L, D_FF, D_MODEL), D_FF ** -0.5),
        "final_g": 1.0 + nrm(ks[19], (D_MODEL,), 0.05),
    }

def reference(x, norm_mix_g, w_in, a_ln_g, a_ln_b, a_ws, a_bs, w_a_out, b_conv, w_b_out,
              rel_bias, w_c_out, d_w, d_scale, w_d_out, w_o, norm_ff_g, w_ff1, w_ff2, final_g):
    B, S, _ = x.shape
    split_at = [sum(IN_SPLITS[:i + 1]) for i in range(len(IN_SPLITS) - 1)]
    for l in range(DEPTH):
        h = rmsnorm(x, norm_mix_g[l])
        z = h @ w_in[l]
        a_u, a_v, b_b, b_c, b_x, c_q, c_k, c_v, d_z, gates = jnp.split(z, split_at, axis=-1)

        y_a = gmlp_spatial_gate(a_u, a_v, a_ln_g[l], a_ln_b[l], a_ws[l], a_bs[l]) @ w_a_out[l]
        y_b = (b_b * causal_short_conv(b_c * b_x, b_conv[l])) @ w_b_out[l]
        y_c = dilated_mixture(c_q, c_k, c_v, rel_bias) @ w_c_out[l]
        y_d = multiscale_pool(d_z, d_w[l], d_scale[l]) @ w_d_out[l]

        g = jax.nn.sigmoid(gates).reshape(B, S, N_BRANCH, D_MODEL)
        merged = (g[:, :, 0] * y_a + g[:, :, 1] * y_b
                  + g[:, :, 2] * y_c + g[:, :, 3] * y_d)
        x = x + merged @ w_o[l]

        h2 = rmsnorm(x, norm_ff_g[l])
        x = x + jnp.square(jax.nn.relu(h2 @ w_ff1[l])) @ w_ff2[l]
    return rmsnorm(x, final_g)


_drawn_inputs = setup_inputs


def setup_inputs(seed=0):
    import zlib

    import numpy as np

    out = dict(_drawn_inputs(seed))
    spreads = {}
    factors = {'a_ln_g': 5.962, 'a_ln_b': 24.985, 'a_bs': 2.712, 'rel_bias': 2.982}
    for name, (base, spread) in spreads.items():
        noise = np.random.default_rng([zlib.crc32(name.encode()), seed]).standard_normal(out[name].shape)
        drawn = base * np.exp(spread * noise) if base else spread * noise
        out[name] = jnp.asarray(drawn.astype(out[name].dtype))
    for name, factor in factors.items():
        out[name] = (out[name] * factor).astype(out[name].dtype)
    return out
```

```python
from contextlib import ExitStack

import numpy as np

import concourse.bass as bass
from concourse import mybir

ALU = mybir.AluOpType
ACT = mybir.ActivationFunctionType
AX = mybir.AxisListType
F32 = mybir.dt.float32
F32R = mybir.dt.float32r

P = 128
D = 1024
S = 1024
KT = D // P
TT = S // P
HALF = 512
NH = S // HALF
WIDTH = 256
BT = WIDTH // P
HEADS = 4
DH = 64
FF = 4 * D
CHUNKS = FF // D
EPS = 1e-6
NEG = -1e30
BUCKETS = 32
DIST = 384
GELU_A, GELU_B = 0.044715, 0.7978845608028654
UNIT = KT * P
GUNIT = UNIT + BT * P
KB = 256

C_GMIX, C_GFF, C_GFIN = 0, 8, 16
C_CONV, C_DSC, C_WINV = 24, 30, 32
C_RATIO = 34
N_COLS = 66

N_QK, N_TM = 6, 8
U_TM = N_QK
U_QK1 = U_TM + N_TM
U_MIX = U_QK1 + N_QK
N_MIX = 10
U_GATE = U_MIX + N_MIX
N_GATE = 4 * KT
U_WO = U_GATE + N_GATE
U_FF = U_WO + KT
N_UNITS = U_FF + 2 * KT * CHUNKS
H_QK1 = 2 * N_QK
H_MIX = 2 * H_QK1
H_GATE = H_MIX + 2 * N_MIX
H_WO = H_GATE + 2 * N_GATE
H_FF = H_WO + 2 * KT
POS_B, POS_A, POS_C, POS_D = 0, 1, 2, 3
GATE_ORDER = (POS_A, POS_C, POS_B, POS_D)
REF_GATE = {POS_A: 0, POS_B: 1, POS_C: 2, POS_D: 3}


def jobs_of(pair):
    return [(hh, part, t) for hh in range(2) for t in range(TT) for part in range(2)]


def build(nc, xT, cols, eye, onehot, rel, lnrow, bsrow, wsT, dw, w1, w2, w3, out):
    ctx = ExitStack()
    with ctx:
        def sb(name, shape, dt=F32):
            return ctx.enter_context(nc.sbuf_tensor(name, shape, dt))

        def sem(name):
            return ctx.enter_context(nc.semaphore(name))

        H = sb("act_split", [P, 2, KT, S], F32R)
        WR = sb("w_raw", [P, 2, GUNIT])
        WH = sb("w_hi", [P, 2, GUNIT], F32R)
        WL = sb("w_lo", [P, 2, GUNIT], F32R)
        rs_b = sb("rs_b", [P, S])
        T = sb("ring", [P, 4, HALF])
        sqacc = sb("sqacc", [P, S])
        cl = sb("cols_sb", [P, N_COLS])
        ident = sb("ident", [P, P])
        ones = sb("ones", [P, P])
        vcol = sb("vcol", [P, 5, TT])
        rs_col = sb("rs_col", [P, 2, TT])
        small = sb("small", [P, TT, 8])

        def place(name, kib, shape, dt=F32):
            with ExitStack() as inner:
                if kib:
                    inner.enter_context(nc.sbuf_tensor(f"below_{name}", [P, int(kib * KB)], F32))
                return inner.enter_context(nc.sbuf_tensor(name, shape, dt))

        Y = place("branch_split", 0, [P, 2, KT, S], F32R)
        M = place("merged", 64, [P, KT, S])
        xs = place("xs", 0, [P, KT, S])
        sq = place("sq", 32, [P, 2, S])
        sqp = place("sq_pool", 40, [P, 2, S])
        onehot_sb = place("onehot_sb", 80, [BUCKETS + 1, 3, DIST])
        rel_sb = place("rel_sb", 90, [BUCKETS + 1, 12])
        dist_sb = place("dist_sb", 85, [HEADS, 3, DIST])
        qk = place("qk", 0, [P, 6, S])
        v12 = place("v12", 24, [P, TT, HALF])
        bias = place("bias", 40, [P, HEADS, 3, WIDTH])
        pts = place("pts", 52, [P, 2, HALF])
        stats = place("stats", 56, [P, P])
        rowsT = place("rowsT", 56.5, [P, P])
        ws_sb = place("ws_sb", 58, [P, 4, P])
        dw_sb = place("dw_sb", 60, [P, BT, P])
        ln_sb = place("ln_sb", 61, [P, 2, WIDTH])
        bs_sb = place("bs_sb", 63, [P, BT, P])
        O = place("attn_out", 64, [P, 2, 2, S])
        va0 = place("va0", 80, [P, TT, HALF])
        R = place("rows", 0, [8, 4, HALF])
        rt = place("row_tmp", 8, [8, 4, HALF])
        wb = place("mix_w", 16, [P, 2, 2, S])
        u = place("gmlp_u", 40, [P, BT, S])
        tc = place("conv_in", 32, [P, BT, S])
        cv = place("conv_out", 64, [P, BT, S])
        z = place("pool_z", 72, [P, BT, S])
        sA = place("pool_a", 0, [P, BT, S])
        sB = place("pool_b", 24, [P, BT, S])

        ps = [ctx.enter_context(nc.psum_tensor(f"bank{i}", [P, HALF], F32)) for i in range(8)]

        dist_dram = nc.dram_tensor("dist_scratch", [3, HEADS, P, DIST], F32, kind="Internal").ap()
        stat_dram = nc.dram_tensor("stat_scratch", [P, P], F32, kind="Internal").ap()
        mixw_dram = nc.dram_tensor("mixw_scratch", [2, HEADS, S], F32, kind="Internal").ap()

        x_in = [sem(f"x_in{k}") for k in range(KT)]
        w_in = [sem(f"w_in{i}") for i in range(2)]
        tab_in, onehot_in, rel_in = sem("tab_in"), sem("onehot_in"), sem("rel_in")
        ones_set, rel_set, dw_zero, ws_masked = sem("ones_set"), sem("rel_set"), sem("dw_zero"), sem("ws_masked")
        w_hi_done, w_split, w_used = sem("w_hi_done"), sem("w_split"), sem("w_used")
        h_hi, h_lo, sq_ready, sq_used = sem("h_hi"), sem("h_lo"), sem("sq_ready"), sem("sq_used")
        ssq_ps, var_ready, std_ready = sem("ssq_ps"), sem("var_ready"), sem("std_ready")
        diag_ready, rsb_ps, rsb_set = sem("diag_ready"), sem("rsb_ps"), sem("rsb_set")
        dist_ps, dist_set, dist_out, bias_in = sem("dist_ps"), sem("dist_set"), sem("dist_out"), sem("bias_in")
        half_done, half_free = sem("half_done"), sem("half_free")
        tmA_done, tmB_done = sem("tmA_done"), sem("tmB_done")
        tm_dve, tm_act = sem("tm_dve"), sem("tm_act")
        s_ready, m_ready, p_ready = sem("s_ready"), sem("m_ready"), sem("p_ready")
        t_ready, t_free, pv_done, o_free = sem("t_ready"), sem("t_free"), sem("pv_done"), sem("o_free")
        statsT_ps, rowsT_set, rows_in = sem("statsT_ps"), sem("rowsT_set"), sem("rows_in")
        rexp_in, rexp_out, mixw_set, mixw_out = (sem(n) for n in ("rexp_in", "rexp_out", "mixw_set", "mixw_out"))
        g_x, g_sq, g_in, g_th = sem("g_x"), sem("g_sq"), sem("g_in"), sem("g_th")
        ln_var, ln_std, v_ready = sem("ln_var"), sem("ln_std"), sem("v_ready")
        sv_done, sv_free = sem("sv_done"), sem("sv_free")
        pool_ready, dmm_done = sem("pool_ready"), sem("dmm_done")
        y_val = [sem(f"y_val{i}") for i in range(4)]
        y_hi = [sem(f"y_hi{i}") for i in range(4)]
        y_lo = [sem(f"y_lo{i}") for i in range(4)]
        tanh_done, y_ps, y_free, m_set = sem("tanh_done"), sem("y_ps"), sem("y_free"), sem("m_set")
        m_hi, m_lo = sem("m_hi"), sem("m_lo")
        xr_in = [sem(f"xr_in{i}") for i in range(2)]
        xg_hi, xg_lo, x2_sq, x2_sum = sem("xg_hi"), sem("xg_lo"), sem("x2_sq"), sem("x2_sum")
        f_hi, f_lo = sem("f_hi"), sem("f_lo")
        x3_sq, x3_g, out_dve, out_pool, out_sent = sem("x3_sq"), sem("x3_g"), sem("out_dve"), sem("out_pool"), sem("out_sent")
        dve_chain, act_chain = sem("dve_chain"), sem("act_chain")
        x3_sum, rs_col_set, ident_in, ws_in, mix_in = (sem(n) for n in ("x3_sum", "rs_col_set", "ident_in", "ws_in", "mix_in"))
        stat_out, wb_in = sem("stat_out"), sem("wb_in")
        pool_sq, pool_sq_part = sem("pool_sq"), sem("pool_sq_part")

        MIX_DMAS = 9
        S_BANKS = (2, 3, 4, 5)

        def zz(q):
            return z[:, q // 2, hs_(q % 2)]

        block = ctx.enter_context(nc.Block())

        def hs_(h):
            return slice(h * HALF, (h + 1) * HALF)

        def strided(t):
            blk, r = divmod(t, 4)
            return slice(blk * HALF + r, (blk + 1) * HALF, 4)

        @block.sync
        def _(sp):
            def weights(src, i, u, n):
                if u >= 2:
                    sp.wait_ge(w_split, u - 1)
                sp.dma_start(WR[:, u % 2, 0:n], src[i]).then_inc(w_in[u % 2], 16)

            sp.dma_start(cl[:], cols).then_inc(tab_in, 16)
            weights(w1, 0, 0, UNIT)
            for k in range(KT):
                sp.dma_start(xs[:, k, :], xT[k * P:(k + 1) * P, :]).then_inc(x_in[k], 16)
            weights(w1, 1, 1, UNIT)
            sp.dma_start(ident[:], eye).then_inc(ident_in, 16)
            sp.dma_start(onehot_sb[:], onehot).then_inc(onehot_in, 16)
            sp.dma_start(rel_sb[0:BUCKETS, :], rel).then_inc(rel_in, 16)
            sp.dma_start(ws_sb[:], wsT).then_inc(ws_in, 16)
            sp.dma_start(ln_sb[:], lnrow.partition_broadcast(P)).then_inc(mix_in, 16)
            sp.wait_ge(dw_zero, 1)
            for g in range(4):
                rows = slice(64 * (g % 2), 64 * (g % 2) + 64)
                sp.dma_start(dw_sb[rows, g // 2, rows], dw[g]).then_inc(mix_in, 16)
                sp.dma_start(bs_sb[rows, g // 2, :], bsrow[g].partition_broadcast(64)).then_inc(mix_in, 16)

            for u_ in range(2, U_GATE):
                weights(w1, u_, u_, UNIT)
            for i in range(N_GATE):
                weights(w2, i, U_GATE + i, GUNIT)
            for i in range(N_UNITS - U_WO):
                weights(w3, i, U_WO + i, UNIT)
            for m in range(KT):
                if m < 6:
                    sp.wait_ge(out_dve, m + 1)
                else:
                    sp.wait_ge(out_pool, m - 5)
                sp.dma_start(out[m * P:(m + 1) * P, :], M[:, m, :]).then_inc(out_sent, 16)
            sp.wait_ge(out_sent, 16 * KT)

        @block.gpsimd
        def _(pool):
            def unit_used(u):
                if u < U_TM:
                    pool.wait_ge(half_done, 2 * u + 2)
                elif u < U_QK1:
                    part, i = divmod(u - U_TM, 4)
                    if i < 3:
                        pool.wait_ge(w_used, 3 * part + i + 1)
                    else:
                        pool.wait_ge(tmB_done if part else tmA_done, TT)
                elif u < U_GATE:
                    pool.wait_ge(half_done, H_QK1 + 2 * (u - U_QK1) + 2)
                elif u < U_WO:
                    pool.wait_ge(y_ps, 2 * (u - U_GATE) + 2)
                else:
                    pool.wait_ge(half_done, H_WO + 2 * (u - U_WO) + 2)

            def split(u, n):
                pool.wait_ge(w_in[u % 2], 16 * (u // 2 + 1))
                if u >= 2:
                    unit_used(u - 2)
                raw, hi, lo = WR[:, u % 2, 0:n], WH[:, u % 2, 0:n], WL[:, u % 2, 0:n]
                pool.tensor_tensor(hi, raw, ones[:, 0:1].to_broadcast([P, n]), ALU.mult).then_inc(w_hi_done, 1)
                pool.wait_ge(w_hi_done, u + 1)
                pool.tensor_tensor(lo, raw, hi.bitcast(F32), ALU.subtract).then_inc(w_split, 1)

            pool.wait_ge(ones_set, 1)
            split(0, UNIT)
            split(1, UNIT)
            for k in range(2):
                pool.wait_ge(x_in[k], 16)
                pool.tensor_tensor(sqp[:, k, :], xs[:, k, :], xs[:, k, :], ALU.mult).then_inc(pool_sq_part, 1)
            pool.wait_ge(pool_sq_part, 2)
            pool.tensor_tensor(sqp[:, 0, :], sqp[:, 0, :], sqp[:, 1, :], ALU.add).then_inc(pool_sq, 1)
            pool.wait_ge(ws_in, 16)
            pool.affine_select(out=ws_sb[:], in_=ws_sb[:], compare_op=ALU.is_ge, fill=0.0, base=0,
                               pattern=[[0, 4], [1, P]], channel_multiplier=-1).then_inc(ws_masked, 1)
            for u_ in range(2, N_UNITS):
                split(u_, GUNIT if U_GATE <= u_ < U_WO else UNIT)
            pool.wait_ge(rsb_set, 3)
            for m in range(6, KT):
                pool.wait_ge(x3_g, 2 * m + 2)
                pool.tensor_tensor(M[:, m, :], M[:, m, :], rs_b[:], ALU.mult).then_inc(out_pool, 1)

        @block.tensor
        def _(pe):
            def split_mm(bank, w, slot, wcol, acts, ak, sl, first, last):
                wh, wl = WH[:, slot, wcol:wcol + P], WL[:, slot, wcol:wcol + P]
                pe.matmul(bank, wh, acts[:, 0, ak, sl], start=first, stop=False)
                pe.matmul(bank, wh, acts[:, 1, ak, sl], start=False, stop=False)
                return pe.matmul(bank, wl, acts[:, 0, ak, sl], start=False, stop=last)

            def bank_of(hs):
                return ps[hs % 4][:]

            def unit(u, hs, acts, before=None, at={}):
                pe.wait_ge(w_split, u + 1)
                for h in range(NH):
                    if hs + h >= 4:
                        pe.wait_ge(half_free, hs + h - 3)
                    for k in range(KT):
                        if before:
                            before(k, h)
                        if (k, h) in at:
                            at[k, h]()
                        mm = split_mm(bank_of(hs + h), WH, u % 2, k * P, acts, k, hs_(h), k == 0, k == KT - 1)
                    mm.then_inc(half_done, 1)

            def sum_squares(ready, n):
                pe.wait_ge(ready, n)
                for h in range(NH):
                    pe.matmul(ps[6 + h][:], ones[:], sqacc[:, hs_(h)], start=True, stop=True).then_inc(ssq_ps, 1)

            def spread_rs(n):
                pe.wait_ge(diag_ready, n + 1)
                for h in range(NH):
                    pe.matmul(ps[6 + h][:], ones[:], T[:, h, :], start=True, stop=True).then_inc(rsb_ps, 1)

            pe.wait_ge(w_split, 1)
            for k in range(KT):
                pe.wait_ge(h_lo, k + 1)
                for h in range(NH):
                    mm = split_mm(bank_of(h), WH, 0, k * P, H, k, hs_(h), k == 0, k == KT - 1)
                    if k == KT - 1:
                        mm.then_inc(half_done, 1)
            pe.wait_ge(ones_set, 1)
            unit(1, 2, H, at={(4, 0): lambda: sum_squares(sq_used, KT - 1)})
            spread_rs(0)
            unit(2, 4, H)
            pe.wait_ge(rsb_set, 1)
            pe.wait_ge(onehot_in, 16)
            pe.wait_ge(rel_set, 1)
            pe.wait_ge(rel_in, 16)
            for g in range(3):
                pe.matmul(ps[5 + g][0:HEADS, 0:DIST], rel_sb[:, g * HEADS:(g + 1) * HEADS],
                          onehot_sb[:, g, :], start=True, stop=True).then_inc(dist_ps, 1)

            for i in range(3, N_QK):
                unit(i, 2 * i, H)
            pe.wait_ge(dist_set, 3)

            for part in range(2):
                for i in range(4):
                    u_ = U_TM + 4 * part + i
                    pe.wait_ge(w_split, u_ + 1)
                    for t in range(TT):
                        if i == 0 and part == 0:
                            if t == 0:
                                pe.wait_ge(half_free, 2 * N_QK)
                                pe.wait_ge(rsb_set, 1)
                        if i == 0 and part == 1:
                            pe.wait_ge(tm_dve if t % 2 else tm_act, t // 2 + 1)
                        toks = slice(t * P, (t + 1) * P) if part == 0 else strided(t)
                        for kk in range(2):
                            k = 2 * i + kk
                            hi, lo = H[:, 0, k, toks], H[:, 1, k, toks]
                            wh, wl = (w[:, u_ % 2, kk * HALF:(kk + 1) * HALF] for w in (WH, WL))
                            pe.matmul(ps[t][:], hi, wh, start=(k == 0), stop=False)
                            pe.matmul(ps[t][:], hi, wl, start=False, stop=False)
                            mm = pe.matmul(ps[t][:], lo, wh, start=False, stop=(k == KT - 1))
                        if i == 3:
                            mm.then_inc(tmB_done if part else tmA_done, 1)
                    if i < 3:
                        mm.then_inc(w_used, 1)

            def attention(pair):
                jobs = jobs_of(pair)
                base = len(jobs) * pair

                def scores(i):
                    n, (hh, part, t) = base + i, jobs[i]
                    if n >= 4:
                        pe.wait_ge(m_ready, n - 3)
                    rows = slice(64 * hh, 64 * hh + DH)
                    bank = ps[S_BANKS[n % 4]]
                    if part == 0:
                        ks = slice(max(t - 1, 0) * P, (t + 1) * P)
                        W = P if t == 0 else 2 * P
                        mm = pe.matmul(bank[:, 0:W], qk[rows, 0, t * P:(t + 1) * P], qk[rows, 1, ks], start=True, stop=True)
                    else:
                        blk, r = divmod(t, 4)
                        W = P * (blk + 1)
                        for g in range(2):
                            mm = pe.matmul(bank[:, g * W:(g + 1) * W], qk[rows, 2 + 2 * g, strided(t)],
                                           qk[rows, 3 + 2 * g, r:(blk + 1) * HALF:4], start=True, stop=True)
                    mm.then_inc(s_ready, 1)

                def turn(i):
                    n, (hh, part, t) = base + i, jobs[i]
                    pe.wait_ge(p_ready, n + 1)
                    if n >= 2:
                        pe.wait_ge(t_free, n - 1)
                    for c in range(len(key_tiles(part, t))):
                        mm = pe.transpose(ps[6 + n % 2][:, c * P:(c + 1) * P], T[:, n % 4, c * P:(c + 1) * P], ident[:])
                    mm.then_inc(t_ready, 1)

                def weighted(i):
                    n, (hh, part, t) = base + i, jobs[i]
                    pe.wait_ge(t_free, n + 1)
                    if n >= 2:
                        pe.wait_ge(o_free, n - 1)
                    head = 2 * pair + hh
                    kts = key_tiles(part, t)
                    for c, (g, kt) in enumerate(kts):
                        v = va0[:, kt, WIDTH + head * DH:WIDTH + (head + 1) * DH] if part == 0 else \
                            v12[:, kt, g * WIDTH + head * DH:g * WIDTH + (head + 1) * DH]
                        mm = pe.matmul(ps[n % 2][64 * hh:64 * hh + DH, 0:P], v, pts[:, n % 2, c * P:(c + 1) * P],
                                       start=(c == 0), stop=(c == len(kts) - 1))
                    mm.then_inc(pv_done, 1)

                for i in range(len(jobs) + 4):
                    if i < len(jobs):
                        scores(i)
                    if 0 <= i - 3 < len(jobs):
                        turn(i - 3)
                    if 0 <= i - 4 < len(jobs):
                        weighted(i - 4)

            pe.wait_ge(tm_dve, TT)
            pe.wait_ge(tm_act, TT)
            pe.wait_ge(half_free, 2 * N_QK)
            attention(0)
            for i in range(N_QK):
                if i == 0:
                    pe.wait_ge(o_free, 32)
                unit(U_QK1 + i, H_QK1 + 2 * i, H)
            pe.wait_ge(half_free, H_MIX)
            attention(1)
            pe.wait_ge(o_free, 64)
            unit(U_MIX, H_MIX, H)
            pe.wait_ge(t_free, 64)
            pe.transpose(ps[7][:, 0:P], stats[:], ident[:]).then_inc(statsT_ps, 1)
            for i in range(1, 8):
                unit(U_MIX + i, H_MIX + 2 * i, H)
            pe.wait_ge(v_ready, 1)
            pe.wait_ge(mix_in, 16 * MIX_DMAS)
            pe.wait_ge(ws_masked, 1)
            pe.wait_ge(rowsT_set, 1)
            for pr in range(BT):
                for h in range(NH):
                    for c in range(4):
                        for gg in range(2):
                            g = 2 * pr + gg
                            mm = pe.matmul(ps[4 + 2 * pr + h][64 * gg:64 * gg + 64, c * P:(c + 1) * P],
                                           va0[:, 4 * h + c, g * 64:(g + 1) * 64], ws_sb[:, g, :], start=True, stop=True)
                    mm.then_inc(sv_done, 1)
            for i in range(8, N_MIX):
                unit(U_MIX + i, H_MIX + 2 * i, H)
            pe.wait_ge(pool_ready, 1)
            pe.wait_ge(sv_free, 4)
            for tile in range(BT):
                for h in range(NH):
                    pe.matmul(ps[4 + 2 * tile + h][:], dw_sb[:, tile, :], z[:, tile, hs_(h)],
                              start=True, stop=True).then_inc(dmm_done, 1)

            for j in range(KT):
                for b, pos in enumerate(GATE_ORDER):
                    i = 4 * j + b
                    u_, hs = U_GATE + i, H_GATE + 2 * i
                    pe.wait_ge(w_split, u_ + 1)
                    for h in range(NH):
                        n = 2 * i + h
                        pe.wait_ge(half_free, hs + h - 3)
                        for k in range(KT):
                            mm = split_mm(bank_of(hs + h), WH, u_ % 2, k * P, H, k, hs_(h), k == 0, k == KT - 1)
                        mm.then_inc(half_done, 1)
                        if n == 0:
                            pe.wait_ge(y_lo[POS_D], 4)
                        if j == 0:
                            pe.wait_ge(y_lo[pos], 2 if pos == POS_C else 4)
                        if n >= 2:
                            pe.wait_ge(y_free, n - 1)
                        for k in range(BT):
                            mm = split_mm(ps[4 + n % 2][:], WH, u_ % 2, UNIT + k * P, Y, 2 * pos + k, hs_(h), k == 0, k == BT - 1)
                        mm.then_inc(y_ps, 1)

            for j in range(KT):
                unit(U_WO + j, H_WO + 2 * j, H,
                     (lambda k, h: pe.wait_ge(m_lo, KT * h + k + 1)) if j == 0 else None)

            for c in range(CHUNKS):
                u_, hs = U_FF + 2 * KT * c, H_FF + 4 * KT * c
                for m in range(KT):
                    unit(u_ + m, hs + 2 * m, Y,
                         (lambda k, h: pe.wait_ge(xg_lo, 2 * k + h + 1)) if c == 0 and m == 0 else None,
                         {(0, 1): lambda: sum_squares(x2_sum, 2 * KT)} if c == 0 and m == 0 else {})
                    if c == 0 and m == 1:
                        spread_rs(1)
                for m in range(KT):
                    unit(u_ + KT + m, hs + 2 * KT + 2 * m, H,
                         (lambda k, h: pe.wait_ge(f_lo, 2 * KT * c + 2 * k + h + 1)) if m == 0 else None)
            sum_squares(x3_sum, 2 * KT)
            spread_rs(2)

        @block.vector
        def _(dve):
            chain = [0]

            def link(ins):
                chain[0] += 1
                ins.then_inc(dve_chain, 1)
                dve.wait_ge(dve_chain, chain[0])

            def norm_factor(n):
                dve.wait_ge(ident_in, 16)
                dve.wait_ge(ssq_ps, 2 * n + 2)
                for c in range(TT):
                    last = dve.tensor_tensor_reduce(out=T[:, 2 + c // 4, (c % 4) * P:(c % 4 + 1) * P], in0=ps[6 + c // 4][:, (c % 4) * P:(c % 4 + 1) * P],
                                                    in1=ident[:], scale=1.0, scalar=0.0, op0=ALU.mult, op1=ALU.add,
                                                    accum_out=vcol[:, 0, c:c + 1])
                link(last)
                dve.tensor_scalar(vcol[:, 1, :], vcol[:, 0, :], 1.0 / D, EPS, ALU.mult, ALU.add).then_inc(var_ready, 1)
                dve.wait_ge(var_ready, n + 1)
                dve.wait_ge(std_ready, n + 1)
                inv_newton(vcol[:, 1, :], rs_col[:, 0, :])
                for c in range(TT):
                    last = dve.tensor_scalar(T[:, c // 4, (c % 4) * P:(c % 4 + 1) * P], ident[:], rs_col[:, 0, c:c + 1], None, ALU.mult)
                last.then_inc(diag_ready, 1)
                dve.wait_ge(rsb_ps, 2 * n + 2)
                for h in range(NH):
                    last = dve.tensor_copy(rs_b[:, hs_(h)], ps[6 + h][:])
                last.then_inc(rsb_set, 1)
                dve.wait_ge(rsb_set, n + 1)

            def inv_newton(var, res):
                link(dve.reciprocal(vcol[:, 3, :], vcol[:, 2, :]))
                link(dve.tensor_tensor(vcol[:, 4, :], vcol[:, 3, :], vcol[:, 3, :], ALU.mult))
                link(dve.tensor_tensor(vcol[:, 4, :], vcol[:, 4, :], var, ALU.mult))
                link(dve.tensor_scalar(vcol[:, 4, :], vcol[:, 4, :], -0.5, 1.5, ALU.mult, ALU.add))
                link(dve.tensor_tensor(res, vcol[:, 3, :], vcol[:, 4, :], ALU.mult))

            def take(hs, dst, then=None):
                dve.wait_ge(half_done, hs + 1)
                h = hs % 2
                return dve.tensor_tensor(dst, ps[hs % 4][:], rs_b[:, hs_(h)], ALU.mult).then_inc(half_free, 1)

            dve.memset(ones[:], 1.0).then_inc(ones_set, 1)
            dve.memset(rel_sb[BUCKETS:BUCKETS + 1, :], NEG).then_inc(rel_set, 1)
            dve.memset(dw_sb[:], 0.0).then_inc(dw_zero, 1)

            dve.wait_ge(tab_in, 16)
            def sum_sq(k):
                dve.wait_ge(sq_ready, k - 1)
                if k == 2:
                    dve.tensor_copy(sqacc[:], sq[:, 0, :]).then_inc(sq_used, 1)
                else:
                    dve.wait_ge(sq_used, k - 2)
                    dve.tensor_tensor(sqacc[:], sqacc[:], sq[:, k % 2, :], ALU.add).then_inc(sq_used, 1)

            for k in range(KT):
                dve.wait_ge(h_hi, k + 1)
                dve.scalar_tensor_tensor(out=H[:, 1, k, :], in0=xs[:, k, :], scalar=cl[:, C_GMIX + k:C_GMIX + k + 1],
                                         in1=H[:, 0, k, :].bitcast(F32), op0=ALU.mult, op1=ALU.subtract).then_inc(h_lo, 1)
                if k >= 3:
                    sum_sq(k - 1)
            sum_sq(KT - 1)
            dve.wait_ge(pool_sq, 1)
            dve.wait_ge(sq_used, KT - 2)
            dve.tensor_tensor(sqacc[:], sqacc[:], sqp[:, 0, :], ALU.add).then_inc(sq_used, 1)
            norm_factor(0)
            for hs in range(4):
                take(hs, qk[:, hs // 2, hs_(hs % 2)])
            for g in range(3):
                dve.wait_ge(dist_ps, g + 1)
                dve.tensor_scalar(dist_sb[:, g, :], ps[5 + g][0:HEADS, 0:DIST], DH ** 0.5, None, ALU.mult).then_inc(dist_set, 1)
            for t in range(TT):
                last = dve.tensor_tensor_reduce(out=T[:, 2 + t // 4, (t % 4) * P:(t % 4 + 1) * P], in0=rs_b[:, strided(t)], in1=ident[:], scale=1.0,
                                                scalar=0.0, op0=ALU.mult, op1=ALU.add, accum_out=rs_col[:, 1, t:t + 1])
            last.then_inc(rs_col_set, 1)
            dve.wait_ge(rs_col_set, 1)
            for hs in range(4, 2 * N_QK):
                take(hs, qk[:, hs // 2, hs_(hs % 2)])
            dve.wait_ge(dist_out, 48)
            for part in range(2):
                for t in range(1, TT, 2):
                    dve.wait_ge(tmB_done if part else tmA_done, t + 1)
                    dve.tensor_scalar((v12 if part else va0)[:, t, :], ps[t][:], rs_col[:, part, t:t + 1], None,
                                      ALU.mult).then_inc(tm_dve, 1)

            def attention(pair):
                jobs = jobs_of(pair)
                base = len(jobs) * pair
                for i in range(len(jobs) + 5):
                    if i < len(jobs):
                        n, (hh, part, t) = base + i, jobs[i]
                        head = 2 * pair + hh
                        W = P * len(key_tiles(part, t))
                        dve.wait_ge(s_ready, n + 1)
                        if n >= 4:
                            dve.wait_ge(t_ready, n - 3)
                        if part == 0:
                            b_ap = bias[:, head, 0, WIDTH - W:WIDTH]
                            o_ap, s_ap = T[:, n % 4, 0:W], ps[S_BANKS[n % 4]][:, 0:W]
                        else:
                            b_ap = bias[:, head, 1:3, WIDTH - W // 2:WIDTH]
                            o_ap, s_ap = (a.rearrange("p (g k) -> p g k", g=2) for a in (T[:, n % 4, 0:W], ps[S_BANKS[n % 4]][:, 0:W]))
                        col = part * 32 + head * TT + t
                        dve.tensor_tensor_reduce(out=o_ap, in0=s_ap, in1=b_ap, scale=-DH ** -0.5, scalar=-NEG, op0=ALU.add,
                                                 op1=ALU.min, accum_out=stats[:, col:col + 1]).then_inc(m_ready, 1)
                    if 0 <= i - 5 < len(jobs):
                        n, (hh, part, t) = base + i - 5, jobs[i - 5]
                        rows = slice(64 * hh, 64 * hh + DH)
                        toks = slice(t * P, (t + 1) * P) if part == 0 else strided(t)
                        dve.wait_ge(pv_done, n + 1)
                        dve.tensor_copy(O[rows, part, pair, toks], ps[n % 2][rows, 0:P]).then_inc(o_free, 1)

            dve.wait_ge(bias_in, 48)
            attention(0)
            def gelu2(n, x):
                r = T[:, n % 4, :]
                if len(x.shape) == 3:
                    r = r.rearrange("p (a b) -> p a b", a=x.shape[1])
                dve.wait_ge(g_sq, n + 1)
                link(dve.tensor_scalar(r, r, GELU_A, 1.0, ALU.mult, ALU.add))
                dve.tensor_tensor(r, r, x, ALU.mult).then_inc(g_in, 1)
                dve.wait_ge(g_th, n + 1)
                link(dve.scalar_tensor_tensor(out=x, in0=r, scalar=1.0, in1=x, op0=ALU.add, op1=ALU.mult))

            def gelu_v(n):
                a = 2 * n
                gelu2(n, va0[:, a:a + 2, 0:WIDTH])

            for i in range(4):
                take(H_QK1 + i, qk[:, i // 2, hs_(i % 2)])
                gelu_v(i)
            for t in range(TT):
                link(dve.bn_stats(small[:, t, 0:6], va0[:, t, 0:WIDTH]))
                last = dve.bn_aggr(small[:, t, 6:8], small[:, t, 0:6])
            link(last)
            dve.tensor_scalar(vcol[:, 1, :], small[:, :, 7], 0.25, EPS, ALU.mult, ALU.add).then_inc(ln_var, 1)
            dve.wait_ge(ln_var, 1)
            dve.wait_ge(ln_std, 1)
            inv_newton(vcol[:, 1, :], vcol[:, 0, :])
            link(dve.tensor_scalar(vcol[:, 0, :], vcol[:, 0, :], 0.5, None, ALU.mult))

            def normed(t):
                v = va0[:, t, 0:WIDTH]
                link(dve.tensor_scalar(v, v, small[:, t, 6:7], vcol[:, 0, t:t + 1], ALU.subtract, ALU.mult))
                link(dve.tensor_tensor(v, v, ln_sb[:, 0, :], ALU.mult))
                return dve.tensor_tensor(v, v, ln_sb[:, 1, :], ALU.add)

            dve.wait_ge(mix_in, 16 * MIX_DMAS)
            for i in range(4, 2 * N_QK):
                take(H_QK1 + i, qk[:, i // 2, hs_(i % 2)])
                last = normed(i - 4)
            last.then_inc(v_ready, 1)
            attention(1)

            def gelu_u(i):
                take(H_MIX + i, u[:, i // 2, hs_(i % 2)])
                dve.wait_ge(half_free, H_MIX + i + 1)
                gelu2(4 + i, u[:, i // 2, hs_(i % 2)])

            gelu_u(0)
            gelu_u(1)
            dve.wait_ge(statsT_ps, 1)
            dve.tensor_copy(rowsT[:], ps[7][:, 0:P]).then_inc(rowsT_set, 1)
            gelu_u(2)
            gelu_u(3)

            dve.wait_ge(rows_in, 16)
            nat = lambda a: a.rearrange("h (p r) -> h p r", r=4)
            per = lambda a: a.rearrange("h (r p) -> h p r", r=4)
            neg0, neg1, den0, den1 = nat(R[:, 0, :]), per(R[:, 1, :]), nat(R[:, 2, :]), per(R[:, 3, :])
            t0, t1, t2, t3 = (nat(rt[:, i, :]) for i in range(4))
            link(dve.tensor_tensor(t2, neg0, neg1, ALU.min))
            dve.tensor_tensor(t0, t2, neg0, ALU.subtract)
            dve.tensor_tensor(t1, t2, neg1, ALU.subtract).then_inc(rexp_in, 1)
            dve.wait_ge(rexp_out, 1)
            dve.tensor_tensor(t2, t0, den0, ALU.mult)
            link(dve.tensor_tensor(t3, t1, den1, ALU.mult))
            link(dve.tensor_tensor(t2, t2, t3, ALU.add))
            link(dve.reciprocal(rt[:, 3, :], rt[:, 2, :]))
            dve.tensor_tensor(t0, t0, t3, ALU.mult)
            dve.tensor_tensor(t1, t1, t3, ALU.mult).then_inc(mixw_set, 1)

            for i in range(4, 8):
                take(H_MIX + i, tc[:, (i - 4) // 2, hs_(i % 2)])
            for i in range(8, 12):
                take(H_MIX + i, T[:, i % 4, :])
                dve.wait_ge(half_free, H_MIX + i + 1)
                x = tc[:, (i - 8) // 2, hs_(i % 2)]
                link(dve.tensor_tensor(x, x, T[:, i % 4, :], ALU.mult))

            def low(pos, n, val, dst, scale=1.0):
                dve.wait_ge(y_hi[pos], n + 1)
                dve.scalar_tensor_tensor(out=Y[:, 1, 2 * pos + dst[0], dst[1]], in0=val, scalar=scale,
                                         in1=Y[:, 0, 2 * pos + dst[0], dst[1]].bitcast(F32),
                                         op0=ALU.mult, op1=ALU.subtract).then_inc(y_lo[pos], 1)

            def attn_mix(pr):
                a, b = O[:, 0, pr, :], O[:, 1, pr, :]
                dve.tensor_tensor(a, a, wb[:, 0, pr, :], ALU.mult)
                link(dve.tensor_tensor(b, b, wb[:, 1, pr, :], ALU.mult))
                dve.tensor_tensor(a, a, b, ALU.add).then_inc(y_val[POS_C], 1)

            def conv(tile):
                c, x = cv[:, tile, :], tc[:, tile, :]
                w = [cl[:, C_CONV + 2 * j + tile:C_CONV + 2 * j + tile + 1] for j in range(3)]
                link(dve.tensor_scalar(c, x, w[2], None, ALU.mult))
                for back in (1, 2):
                    link(dve.scalar_tensor_tensor(out=c[:, back:S], in0=x[:, 0:S - back], scalar=w[2 - back],
                                                  in1=c[:, back:S], op0=ALU.mult, op1=ALU.add))

            dve.wait_ge(wb_in, 16 * 8)
            attn_mix(0)
            attn_mix(1)
            dve.wait_ge(y_val[POS_C], 2)
            take(H_MIX + 12, zz(0))
            take(H_MIX + 13, zz(1))
            low(POS_C, 0, O[:, 0, 0, :], (0, slice(0, S)))
            take(H_MIX + 14, zz(2))
            low(POS_C, 1, O[:, 0, 1, :], (1, slice(0, S)))
            dve.wait_ge(y_lo[POS_C], 2)
            take(H_MIX + 15, zz(3))
            dve.wait_ge(half_free, H_MIX + 16)
            conv(0)
            conv(1)

            def doubled(dst, src, back, tiles, rows):
                d, s = dst[rows, tiles, :], src[rows, tiles, :]
                dve.tensor_copy(d[:, :, 0:back], s[:, :, 0:back])
                link(dve.tensor_tensor(d[:, :, back:S], s[:, :, back:S], s[:, :, 0:S - back], ALU.add))

            both, all_rows, upper = slice(0, BT), slice(0, P), slice(64, P)
            doubled(sA, z, 1, both, all_rows)
            doubled(sB, sA, 2, both, all_rows)
            doubled(sA, sB, 4, slice(1, 2), all_rows)
            doubled(sB, sA, 8, slice(1, 2), upper)
            for tile in range(BT):
                ratio = cl[:, C_RATIO + 16 * tile:C_RATIO + 16 * (tile + 1)]
                for rows, sums in ((slice(0, 64), sA), (upper, sB)):
                    s = sums[rows, tile, :]
                    link(dve.tensor_tensor(s[:, 0:16], s[:, 0:16], ratio[rows, :], ALU.mult))
                    last = dve.scalar_tensor_tensor(out=z[rows, tile, :], in0=s, scalar=cl[rows, C_WINV + tile:C_WINV + tile + 1],
                                                    in1=z[rows, tile, :], op0=ALU.mult, op1=ALU.subtract)
            last.then_inc(pool_ready, 1)

            def piece(q):
                return q // 2, hs_(q % 2)

            for q in range(5):
                if q < 4:
                    dve.wait_ge(sv_done, q + 1)
                    r = T[:, q, :].rearrange("p (c t) -> p c t", c=4)
                    dve.tensor_tensor(r, ps[4 + q][:].rearrange("p (c t) -> p c t", c=4),
                                      bs_sb[:, q // 2, :].unsqueeze(1).to_broadcast([P, 4, P]), ALU.add).then_inc(sv_free, 1)
                    dve.wait_ge(sv_free, q + 1)
                    x = u[:, q // 2, hs_(q % 2)]
                    dve.tensor_tensor(x, x, T[:, q, :], ALU.mult).then_inc(y_val[POS_A], 1)
                if q >= 1:
                    low(POS_A, q - 1, u[:, (q - 1) // 2, hs_((q - 1) % 2)], piece(q - 1), 0.5)

            for q in range(5):
                if q < 4:
                    take(H_MIX + 16 + q, T[:, q, :])
                    dve.wait_ge(half_free, H_MIX + 16 + q + 1)
                    x = cv[:, q // 2, hs_(q % 2)]
                    dve.tensor_tensor(x, x, T[:, q, :], ALU.mult).then_inc(y_val[POS_B], 1)
                if q >= 1:
                    low(POS_B, q - 1, cv[:, (q - 1) // 2, hs_((q - 1) % 2)], piece(q - 1))

            dve.wait_ge(dmm_done, 4)
            for q in range(4):
                low(POS_D, q, ps[4 + q][:], piece(q), cl[:, C_DSC + q // 2:C_DSC + q // 2 + 1])

            def gate_terms(n):
                j, b, h = n // 8, n // 2 % 4, n % 2
                dve.wait_ge(tanh_done, n + 1)
                dve.wait_ge(y_ps, n + 1)
                r, m = T[:, n % 4, :], M[:, j, hs_(h)]
                ins = dve.scalar_tensor_tensor(out=m if b == 0 else r, in0=r, scalar=1.0, in1=ps[4 + n % 2][:],
                                               op0=ALU.add, op1=ALU.mult).then_inc(y_free, 1)
                if b:
                    dve.wait_ge(y_free, n + 1)
                    ins = dve.tensor_tensor(m, m, r, ALU.add)
                if b == 3:
                    ins.then_inc(m_set, 1)

            for n in range(2 * N_GATE):
                take(H_GATE + n, T[:, n % 4, :])
                if n >= 1:
                    gate_terms(n - 1)
            for n in range(2 * KT):
                if n == 2:
                    gate_terms(2 * N_GATE - 1)
                h, k = divmod(n, KT)
                dve.wait_ge(m_hi, n + 1)
                dve.scalar_tensor_tensor(out=H[:, 1, k, hs_(h)], in0=M[:, k, hs_(h)], scalar=0.5,
                                         in1=H[:, 0, k, hs_(h)].bitcast(F32), op0=ALU.mult, op1=ALU.subtract).then_inc(m_lo, 1)

            def acc_sq(n, ready, done):
                dve.wait_ge(ready, n + 1)
                a = sqacc[:, hs_(n % 2)]
                if n < 2:
                    dve.tensor_copy(a, T[:, n % 2, :]).then_inc(done, 1)
                else:
                    dve.wait_ge(done, n - 1)
                    dve.tensor_tensor(a, a, T[:, n % 2, :], ALU.add).then_inc(done, 1)

            for n in range(2 * KT + 1):
                if n < 2 * KT:
                    j, h = n // 2, n % 2
                    dve.wait_ge(xr_in[n % 2], 16 * (n // 2 + 1))
                    dve.wait_ge(half_done, H_WO + n + 1)
                    dve.tensor_tensor(M[:, j, hs_(h)], ps[n % 4][:], T[:, 2 + n % 2, :], ALU.add).then_inc(half_free, 1)
                if n >= 1:
                    j, h = (n - 1) // 2, (n - 1) % 2
                    dve.wait_ge(xg_hi, n)
                    dve.scalar_tensor_tensor(out=Y[:, 1, j, hs_(h)], in0=M[:, j, hs_(h)], scalar=cl[:, C_GFF + j:C_GFF + j + 1],
                                             in1=Y[:, 0, j, hs_(h)].bitcast(F32), op0=ALU.mult, op1=ALU.subtract).then_inc(xg_lo, 1)
                    acc_sq(n - 1, x2_sq, x2_sum)
            norm_factor(1)

            for c in range(CHUNKS):
                for n in range(2 * KT + 1):
                    if n < 2 * KT:
                        hs = H_FF + 4 * KT * c + n
                        dve.wait_ge(half_done, hs + 1)
                        dve.scalar_tensor_tensor(out=T[:, n % 4, :], in0=ps[hs % 4][:], scalar=0.0, in1=rs_b[:, hs_(n % 2)],
                                                 op0=ALU.max, op1=ALU.mult).then_inc(half_free, 1)
                    if n >= 1:
                        m, h = (n - 1) // 2, (n - 1) % 2
                        dve.wait_ge(f_hi, 2 * KT * c + n)
                        dve.tensor_tensor(H[:, 1, m, hs_(h)], T[:, (n - 1) % 4, :], H[:, 0, m, hs_(h)].bitcast(F32),
                                          ALU.subtract).then_inc(f_lo, 1)
                for n in range(2 * KT + 1):
                    if n < 2 * KT:
                        hs = H_FF + 4 * KT * c + 2 * KT + n
                        m = M[:, n // 2, hs_(n % 2)]
                        dve.wait_ge(half_done, hs + 1)
                        dve.tensor_tensor(m, m, ps[hs % 4][:], ALU.add).then_inc(half_free, 1)
                    if n >= 1 and c == CHUNKS - 1:
                        acc_sq(n - 1, x3_sq, x3_sum)
            norm_factor(2)
            for m in range(6):
                dve.wait_ge(x3_g, 2 * m + 2)
                dve.tensor_tensor(M[:, m, :], M[:, m, :], rs_b[:], ALU.mult).then_inc(out_dve, 1)

        @block.scalar
        def _(act):
            chain = [0]

            def link(ins):
                chain[0] += 1
                ins.then_inc(act_chain, 1)
                act.wait_ge(act_chain, chain[0])

            def root(n, src, ready, done):
                act.wait_ge(ready, n + 1)
                act.activation(vcol[:, 2, :], src, ACT.Sqrt).then_inc(done, 1)

            act.wait_ge(ones_set, 1)
            act.activation(vcol[:, 4, 0:1], ones[:, 0:1], ACT.Sqrt)
            act.wait_ge(tab_in, 16)
            for k in range(KT):
                act.wait_ge(x_in[k], 16)
                act.activation(H[:, 0, k, :], xs[:, k, :], ACT.Copy, scale=cl[:, C_GMIX + k:C_GMIX + k + 1]).then_inc(h_hi, 1)
                if k >= 2:
                    if k >= 4:
                        act.wait_ge(sq_used, k - 3)
                    act.activation(sq[:, k % 2, :], xs[:, k, :], ACT.Square).then_inc(sq_ready, 1)
            root(0, vcol[:, 1, :], var_ready, std_ready)
            act.wait_ge(dist_set, 3)
            for g in range(3):
                act.dma_start(dist_dram[g], dist_sb[:, g, :].unsqueeze(1).to_broadcast([HEADS, P, DIST])).then_inc(dist_out, 16)
            act.wait_ge(dist_out, 48)
            for t in range(0, TT, 2):
                act.wait_ge(tmA_done, t + 1)
                act.wait_ge(rs_col_set, 1)
                act.activation(va0[:, t, :], ps[t][:], ACT.Copy, scale=rs_col[:, 0, t:t + 1]).then_inc(tm_act, 1)
            for g in range(3):
                toeplitz = dist_dram[g].rearrange("h p d -> h (p d)")[:, P - 1:P - 1 + P * (DIST - 1)]
                toeplitz = toeplitz.rearrange("h (p d) -> p h d", d=DIST - 1)[:, :, 0:WIDTH]
                act.dma_start(bias[:, :, g, :], toeplitz).then_inc(bias_in, 16)
            for t in range(0, TT, 2):
                act.wait_ge(tmB_done, t + 1)
                act.activation(v12[:, t, :], ps[t][:], ACT.Copy, scale=rs_col[:, 1, t:t + 1]).then_inc(tm_act, 1)

            def attention(pair):
                jobs = jobs_of(pair)
                base = len(jobs) * pair
                for i in range(len(jobs) + 3):
                    if 0 <= i - 1 < len(jobs):
                        n, (hh, part, t) = base + i - 1, jobs[i - 1]
                        W = P * len(key_tiles(part, t))
                        col = part * 32 + (2 * pair + hh) * TT + t
                        act.wait_ge(m_ready, n + 1)
                        act.activation(T[:, n % 4, 0:W], T[:, n % 4, 0:W], ACT.Exp, scale=-1.0, bias=stats[:, col:col + 1],
                                       accum_out=stats[:, 64 + col:65 + col]).then_inc(p_ready, 1)
                    if 0 <= i - 3 < len(jobs):
                        n, (hh, part, t) = base + i - 3, jobs[i - 3]
                        W = P * len(key_tiles(part, t))
                        act.wait_ge(t_ready, n + 1)
                        if n >= 2:
                            act.wait_ge(pv_done, n - 1)
                        act.activation(pts[:, n % 2, 0:W], ps[6 + n % 2][:, 0:W], ACT.Copy).then_inc(t_free, 1)

            attention(0)

            def gelu2(n, x):
                r = T[:, n % 4, :]
                if len(x.shape) == 3:
                    r = r.rearrange("p (a b) -> p a b", a=x.shape[1])
                act.activation(r, x, ACT.Square).then_inc(g_sq, 1)
                act.wait_ge(g_in, n + 1)
                act.activation(r, r, ACT.Tanh, scale=GELU_B).then_inc(g_th, 1)

            for n in range(4):
                gelu2(n, va0[:, 2 * n:2 * n + 2, 0:WIDTH])
            root(0, vcol[:, 1, :], ln_var, ln_std)
            attention(1)

            def gelu_u(i):
                act.wait_ge(half_free, H_MIX + i + 1)
                gelu2(4 + i, u[:, i // 2, hs_(i % 2)])

            gelu_u(0)
            gelu_u(1)
            act.wait_ge(rowsT_set, 1)
            act.dma_start(stat_dram, rowsT[:]).then_inc(stat_out, 16)
            gelu_u(2)
            gelu_u(3)
            act.wait_ge(stat_out, 16)
            act.dma_start(R[:], stat_dram.rearrange("(s hb t) q -> hb s (t q)", s=4, hb=8)).then_inc(rows_in, 16)
            act.wait_ge(rexp_in, 1)
            act.activation(rt[:, 0:2, :], rt[:, 0:2, :], ACT.Exp).then_inc(rexp_out, 1)
            act.wait_ge(mixw_set, 1)
            for part in range(2):
                act.dma_start(mixw_dram[part].rearrange("h (b t) -> (h b) t", b=2), rt[:, part, :]).then_inc(mixw_out, 16)
            act.wait_ge(mixw_out, 32)
            for part in range(2):
                for head in range(HEADS):
                    rows = slice(64 * (head % 2), 64 * (head % 2) + 64)
                    act.dma_start(wb[rows, part, head // 2, :], mixw_dram[part, head].partition_broadcast(64)).then_inc(wb_in, 16)

            def high(pos, n, ready, val, dst, scale=1.0):
                act.wait_ge(ready, n + 1)
                act.activation(Y[:, 0, 2 * pos + dst[0], dst[1]], val, ACT.Copy, scale=scale).then_inc(y_hi[pos], 1)

            for pr in range(BT):
                if pr == 0:
                    act.wait_ge(y_val[POS_C], 2)
                high(POS_C, pr, y_val[POS_C], O[:, 0, pr, :], (pr, slice(0, S)))
            for q in range(4):
                high(POS_A, q, y_val[POS_A], u[:, q // 2, hs_(q % 2)], (q // 2, hs_(q % 2)), 0.5)
            for q in range(4):
                high(POS_B, q, y_val[POS_B], cv[:, q // 2, hs_(q % 2)], (q // 2, hs_(q % 2)))
            for q in range(4):
                high(POS_D, q, dmm_done, ps[4 + q][:], (q // 2, hs_(q % 2)), cl[:, C_DSC + q // 2:C_DSC + q // 2 + 1])

            for n in range(2 * N_GATE):
                act.wait_ge(half_free, H_GATE + n + 1)
                act.activation(T[:, n % 4, :], T[:, n % 4, :], ACT.Tanh, scale=0.5).then_inc(tanh_done, 1)

            def reload_x(n):
                if n >= 2:
                    act.wait_ge(half_free, H_WO + n - 1)
                act.dma_start(T[:, 2 + n % 2, :], xT[(n // 2) * P:(n // 2 + 1) * P, hs_(n % 2)]).then_inc(xr_in[n % 2], 16)

            act.wait_ge(m_set, 2 * KT - 2)
            for n in range(2 * KT):
                h, k = divmod(n, KT)
                if n == KT - 1:
                    act.wait_ge(m_set, 2 * KT)
                    reload_x(0)
                    reload_x(1)
                act.activation(H[:, 0, k, hs_(h)], M[:, k, hs_(h)], ACT.Copy, scale=0.5).then_inc(m_hi, 1)
            for n in range(2 * KT):
                j, h = n // 2, n % 2
                act.wait_ge(half_free, H_WO + n + 1)
                act.activation(Y[:, 0, j, hs_(h)], M[:, j, hs_(h)], ACT.Copy, scale=cl[:, C_GFF + j:C_GFF + j + 1]).then_inc(xg_hi, 1)
                if n >= 2:
                    act.wait_ge(x2_sum, n - 1)
                act.activation(T[:, n % 2, :], M[:, j, hs_(h)], ACT.Square).then_inc(x2_sq, 1)
                if n + 2 < 2 * KT:
                    reload_x(n + 2)
            root(1, vcol[:, 1, :], var_ready, std_ready)

            for c in range(CHUNKS):
                for n in range(2 * KT):
                    act.wait_ge(half_free, H_FF + 4 * KT * c + n + 1)
                    r = T[:, n % 4, :]
                    link(act.activation(r, r, ACT.Square))
                    act.activation(H[:, 0, n // 2, hs_(n % 2)], r, ACT.Copy).then_inc(f_hi, 1)
            for n in range(2 * KT):
                m = M[:, n // 2, hs_(n % 2)]
                act.wait_ge(half_free, H_FF + 4 * KT * (CHUNKS - 1) + 2 * KT + n + 1)
                if n >= 2:
                    act.wait_ge(x3_sum, n - 1)
                act.activation(T[:, n % 2, :], m, ACT.Square).then_inc(x3_sq, 1)
                act.activation(m, m, ACT.Copy, scale=cl[:, C_GFIN + n // 2:C_GFIN + n // 2 + 1]).then_inc(x3_g, 1)
            root(2, vcol[:, 1, :], var_ready, std_ready)


def key_tiles(part, t):
    if part == 0:
        return [(0, k) for k in range(max(t - 1, 0), t + 1)]
    blk, r = divmod(t, 4)
    return [(g, 4 * b + r) for g in range(2) for b in range(blk + 1)]


def t5_bucket(dist):
    exact = BUCKETS // 2
    d = np.maximum(dist, 1).astype(np.float32)
    large = exact + (np.log(d / np.float32(exact)) / np.float32(np.log(2048 / exact)) * (BUCKETS - exact)).astype(np.int32)
    return np.where(dist < exact, dist, np.minimum(large, BUCKETS - 1))


def distance_onehot():
    e = np.zeros((BUCKETS + 1, 3, DIST), np.float32)
    for g, dil in enumerate((1, 4, 16)):
        for i in range(DIST):
            diff = 255 - i
            step = 4 if g == 2 else 1
            ok = 0 <= diff <= P * step and diff % step == 0
            row = int(t5_bucket(np.array(diff // step * dil))) if ok else BUCKETS
            e[row, g, i] = 1.0
    return e


def kernel(**inputs):
    import concourse.bacc as bacc
    from concourse.bass_utils import run_bass_kernel_spmd as run

    a = {k: np.asarray(v) for k, v in inputs.items()}
    w_in = a["w_in"][0]
    cuts = np.cumsum([0, WIDTH, WIDTH, WIDTH, WIDTH, WIDTH, 768, 768, 768, WIDTH])
    A_U, A_V, B_B, B_C, B_X, C_Q, C_K, C_V, D_Z, GATES = (int(x) for x in cuts)

    def block(w, c):
        return w[:, c:c + P].reshape(-1, P, P).transpose(1, 0, 2).reshape(P, -1)

    units = []
    for pair in range(2):
        qk = [block(w_in, base + g * WIDTH + pair * P) for g in range(3) for base in (C_Q, C_K)]
        units += qk
        if pair == 0:
            for wide in (np.concatenate([w_in[:, A_V:A_V + WIDTH], w_in[:, C_V:C_V + WIDTH]], 1),
                         w_in[:, C_V + WIDTH:C_V + 3 * WIDTH]):
                units += [w.transpose(1, 0, 2).reshape(P, UNIT) for w in wide.reshape(4, 2, P, HALF)]
    units += [block(w_in, base + m * P) for base in (A_U, B_C, B_X, D_Z, B_B) for m in range(BT)]
    w1 = np.stack(units)
    outs = {POS_A: a["w_a_out"][0], POS_B: a["w_b_out"][0], POS_C: a["w_c_out"][0], POS_D: a["w_d_out"][0]}
    w2 = np.stack([np.concatenate([block(w_in, GATES + REF_GATE[pos] * D + j * P), block(outs[pos], j * P)], 1)
                   for j in range(KT) for pos in GATE_ORDER])
    f1, f2 = a["w_ff1"][0], a["w_ff2"][0]
    units = [block(a["w_o"][0], j * P) for j in range(KT)]
    for c in range(CHUNKS):
        units += [block(f1, c * D + m * P) for m in range(KT)]
        units += [block(f2[c * D:(c + 1) * D], m * P) for m in range(KT)]
    w3 = np.stack(units)

    cols = np.zeros((P, N_COLS), np.float32)
    cols[:, C_GMIX:C_GMIX + KT] = a["norm_mix_g"][0].reshape(KT, P).T
    cols[:, C_GFF:C_GFF + KT] = a["norm_ff_g"][0].reshape(KT, P).T
    cols[:, C_GFIN:C_GFIN + KT] = a["final_g"].reshape(KT, P).T
    cols[:, C_CONV:C_CONV + 6] = a["b_conv"][0].reshape(3 * BT, P).T
    cols[:, C_DSC:C_DSC + BT] = a["d_scale"][0].reshape(BT, P).T
    windows = np.repeat(np.array([2, 4, 8, 16], np.float32), 64).reshape(BT, P)
    cols[:, C_WINV:C_WINV + BT] = (1 / windows).T
    t = np.arange(1, 17, dtype=np.float32)
    cols[:, C_RATIO:] = (windows[:, :, None] / np.minimum(t, windows[:, :, None])).transpose(1, 0, 2).reshape(P, -1)

    arrays = {
        "xT": np.ascontiguousarray(a["x"][0].T), "cols": cols, "eye": np.eye(P, dtype=np.float32),
        "onehot": distance_onehot(), "rel": a["rel_bias"],
        "lnrow": np.stack([a["a_ln_g"][0], a["a_ln_b"][0]]), "bsrow": a["a_bs"][0],
        "wsT": np.ascontiguousarray(a["a_ws"][0].transpose(2, 0, 1)), "dw": a["d_w"][0],
        "w1": w1, "w2": w2, "w3": w3,
    }
    nc = bacc.Bacc("TRN2", target_bir_lowering=False, num_devices=1)
    aps = [nc.dram_tensor(f"in_{n}", v.shape, mybir.dt.from_np(v.dtype), kind="ExternalInput").ap() for n, v in arrays.items()]
    outT = nc.dram_tensor("outT", (D, S), F32, kind="ExternalOutput").ap()
    build(nc, *aps, outT)
    r = run(nc, [{f"in_{n}": v for n, v in arrays.items()}], core_ids=[0])
    return r.results[0]["outT"].T.reshape(1, S, D)
```

```python
from contextlib import ExitStack

import numpy as np

import concourse.bass as bass
from concourse import mybir

ALU = mybir.AluOpType
ACT = mybir.ActivationFunctionType
AX = mybir.AxisListType
F32 = mybir.dt.float32
F32R = mybir.dt.float32r

P = 128
D = 1024
S = 1024
KT = D // P
TT = S // P
HALF = 512
NH = S // HALF
WIDTH = 256
BT = WIDTH // P
HEADS = 4
DH = 64
FF = 4 * D
CHUNKS = FF // D
EPS = 1e-6
NEG = -1e30
BUCKETS = 32
DIST = 384
GELU_A, GELU_B = 0.044715, 0.7978845608028654
UNIT = KT * P
GUNIT = UNIT + BT * P
KB = 256

C_GMIX, C_GFF, C_GFIN = 0, 8, 16
C_CONV, C_DSC, C_WINV = 24, 30, 32
C_RATIO = 34
N_COLS = 66

N_QK, N_TM = 6, 8
U_TM = N_QK
U_QK1 = U_TM + N_TM
U_MIX = U_QK1 + N_QK
N_MIX = 10
U_GATE = U_MIX + N_MIX
N_GATE = 4 * KT
U_WO = U_GATE + N_GATE
U_FF = U_WO + KT
N_UNITS = U_FF + 2 * KT * CHUNKS
H_QK1 = 2 * N_QK
H_MIX = 2 * H_QK1
H_GATE = H_MIX + 2 * N_MIX
H_WO = H_GATE + 2 * N_GATE
H_FF = H_WO + 2 * KT
OUT_POOL = ((0, 1, 2, 3, 4), (0, 1, 2))
OUT_DVE = tuple(tuple(m for m in range(KT) if m not in tiles) for tiles in OUT_POOL)
OUT_SENT = [(0, m) for m in (0, 5, 1, 6, 2, 3, 7, 4)] + [(1, m) for m in OUT_DVE[1]]
POOL_LOWS = (2, 4, 6)
DVE_LOWS = [(h, k) for h in range(NH) for k in range(KT) if h or k not in POOL_LOWS]
POS_B, POS_A, POS_D, POS_C = 0, 1, 2, 3
GATE_ORDER = (POS_A, POS_B, POS_D, POS_C)
REF_GATE = {POS_A: 0, POS_B: 1, POS_C: 2, POS_D: 3}


def jobs_of(pair):
    return [(hh, part, t) for hh in range(2) for t in range(TT) for part in range(2)]


def build(nc, xT, cols, eye, onehot, rel, lnrow, bsrow, wsT, dw, w1, w2, w3, out):
    ctx = ExitStack()
    with ctx:
        def sb(name, shape, dt=F32):
            return ctx.enter_context(nc.sbuf_tensor(name, shape, dt))

        def sem(name):
            return ctx.enter_context(nc.semaphore(name))

        H = sb("act_split", [P, 2, KT, S], F32R)
        WR = sb("w_raw", [P, 2, GUNIT])
        WH = sb("w_hi", [P, 2, GUNIT], F32R)
        WL = sb("w_lo", [P, 2, GUNIT], F32R)
        rs_b = sb("rs_b", [P, S])
        with ExitStack() as inner:
            diag = inner.enter_context(nc.sbuf_tensor("diagonals", [P, 4, HALF], F32R))
        T = sb("ring", [P, 4, HALF])
        sqacc = sb("sqacc", [P, S])
        cl = sb("cols_sb", [P, N_COLS])
        ident = sb("ident", [P, P])
        ones = sb("ones", [P, 1])
        ones_r = sb("ones_r", [P, P], F32R)
        vcol = sb("vcol", [P, 5, 2 * TT])
        rs_hi = sb("rs_hi", [P, 2 * TT], F32R)
        rs_lo = sb("rs_lo", [P, 2 * TT], F32R)
        rs_col = sb("rs_col", [P, 2 * TT])

        def place(name, kib, shape, dt=F32):
            with ExitStack() as inner:
                if kib:
                    inner.enter_context(nc.sbuf_tensor(f"below_{name}", [P, int(kib * KB)], F32))
                return inner.enter_context(nc.sbuf_tensor(name, shape, dt))

        Y = place("branch_split", 0, [P, 2, KT, S], F32R)
        M = place("merged", 64, [P, KT, S])
        xs = place("xs", 0, [P, KT, S])
        sq = place("sq", 32, [P, 2, S])
        sqp = place("sq_pool", 40, [P, 2, S])
        onehot_sb = place("onehot_sb", 80, [BUCKETS + 1, 3, DIST])
        rel_sb = place("rel_sb", 90, [BUCKETS + 1, 12])
        dist_sb = place("dist_sb", 85, [HEADS, 3, DIST])
        qk = place("qk", 0, [P, 6, S])
        v12 = place("v12", 24, [P, TT, HALF])
        bias = place("bias", 40, [P, HEADS, 3, WIDTH])
        pts = place("pts", 52, [P, 2, HALF])
        stats = place("stats", 56, [P, P])
        rowsT = place("rowsT", 56.5, [P, P])
        small = place("ln_stats", 57, [P, TT, 8])
        ws_sb = place("ws_sb", 58, [P, 4, P])
        dw_sb = place("dw_sb", 60, [P, BT, P])
        ln_sb = place("ln_sb", 61, [P, 2, WIDTH])
        bs_sb = place("bs_sb", 63, [P, BT, P])
        O = place("attn_out", 64, [P, 2, 2, S])
        va0 = place("va0", 80, [P, TT, HALF])
        R = place("rows", 0, [8, 4, HALF])
        rt = place("row_tmp", 8, [8, 2, HALF])
        sA = place("pool_a", 12, [P, S])
        wb = place("mix_w", 16, [P, 2, 2, S])
        u = place("gmlp_u", 40, [P, BT, S])
        tc = place("conv_in", 32, [P, BT, S])
        cv = place("conv_out", 72, [P, BT, S])
        z = place("pool_z", 48, [P, BT, S])

        ps = [ctx.enter_context(nc.psum_tensor(f"bank{i}", [P, HALF], F32)) for i in range(8)]

        dist_dram = nc.dram_tensor("dist_scratch", [3, HEADS, P, DIST], F32, kind="Internal").ap()
        stat_dram = nc.dram_tensor("stat_scratch", [P, P], F32, kind="Internal").ap()
        mixw_dram = nc.dram_tensor("mixw_scratch", [2, HEADS, S], F32, kind="Internal").ap()

        x_in = [sem(f"x_in{k}") for k in range(KT)]
        w_in = [sem(f"w_in{i}") for i in range(2)]
        tab_in, onehot_in, rel_in = sem("tab_in"), sem("onehot_in"), sem("rel_in")
        ones_set, rel_set, dw_zero, ws_masked = sem("ones_set"), sem("rel_set"), sem("dw_zero"), sem("ws_masked")
        w_hi_done, w_split, w_used = sem("w_hi_done"), sem("w_split"), sem("w_used")
        h_hi, h_lo, sq_ready, sq_used = sem("h_hi"), sem("h_lo"), sem("sq_ready"), sem("sq_used")
        ssq_ps, var_ready, std_ready = sem("ssq_ps"), sem("var_ready"), sem("std_ready")
        diag_ready, rsb_ps, rsb_set = sem("diag_ready"), sem("rsb_ps"), sem("rsb_set")
        dist_ps, dist_set, dist_out, bias_in = sem("dist_ps"), sem("dist_set"), sem("dist_out"), sem("bias_in")
        half_done, half_free = sem("half_done"), sem("half_free")
        tmA_done, tmB_done = sem("tmA_done"), sem("tmB_done")
        tm_dve, tm_act = sem("tm_dve"), sem("tm_act")
        s_ready, m_ready, p_ready = sem("s_ready"), sem("m_ready"), sem("p_ready")
        t_ready, t_free, pv_done, o_free = sem("t_ready"), sem("t_free"), sem("pv_done"), sem("o_free")
        statsT_ps, rowsT_set, rows_in = sem("statsT_ps"), sem("rowsT_set"), sem("rows_in")
        rexp_in, rexp_out, mixw_set, mixw_out = (sem(n) for n in ("rexp_in", "rexp_out", "mixw_set", "mixw_out"))
        g_x, g_sq, g_in, g_th = sem("g_x"), sem("g_sq"), sem("g_in"), sem("g_th")
        ln_var, ln_std, v_ready = sem("ln_var"), sem("ln_std"), sem("v_ready")
        sv_done, sv_free = sem("sv_done"), sem("sv_free")
        pool_ready, dmm_done = sem("pool_ready"), sem("dmm_done")
        y_val = [sem(f"y_val{i}") for i in range(4)]
        y_hi = [sem(f"y_hi{i}") for i in range(4)]
        y_lo = [sem(f"y_lo{i}") for i in range(4)]
        tanh_done, y_ps, y_free, m_set = sem("tanh_done"), sem("y_ps"), sem("y_free"), sem("m_set")
        m_hi, m_lo, m_lo_pool = sem("m_hi"), sem("m_lo"), sem("m_lo_pool")
        xr_in = [sem(f"xr_in{i}") for i in range(2)]
        xg_hi, xg_lo, x2_sq, x2_sum = sem("xg_hi"), sem("xg_lo"), sem("x2_sq"), sem("x2_sum")
        f_hi, f_lo = sem("f_hi"), sem("f_lo")
        x3_sq, x3_g, out_dve, out_pool, out_sent = sem("x3_sq"), sem("x3_g"), sem("out_dve"), sem("out_pool"), sem("out_sent")
        dve_chain, act_chain = sem("dve_chain"), sem("act_chain")
        x3_sum, ident_in, ws_in, mix_in = (sem(n) for n in ("x3_sum", "ident_in", "ws_in", "mix_in"))
        stat_out, wb_in = sem("stat_out"), sem("wb_in")
        pool_sq, pool_sq_part = sem("pool_sq"), sem("pool_sq_part")

        MIX_DMAS = 9
        S_BANKS = (2, 3, 4, 5)

        def bank_of(hs):
            return ps[hs % 6 if hs < H_QK1 else (hs + 2) % 4][:]

        def zz(q):
            return z[:, q // 2, hs_(q % 2)]

        block = ctx.enter_context(nc.Block())

        def hs_(h):
            return slice(h * HALF, (h + 1) * HALF)

        def strided(t):
            blk, r = divmod(t, 4)
            return slice(blk * HALF + r, (blk + 1) * HALF, 4)

        @block.sync
        def _(sp):
            def weights(src, i, u, n):
                if u >= 2:
                    sp.wait_ge(w_split, u - 1)
                sp.dma_start(WR[:, u % 2, 0:n], src[i]).then_inc(w_in[u % 2], 16)

            sp.dma_start(cl[:], cols).then_inc(tab_in, 16)
            weights(w1, 0, 0, UNIT)
            for k in range(KT):
                sp.dma_start(xs[:, k, :], xT[k * P:(k + 1) * P, :]).then_inc(x_in[k], 16)
                if k == 2:
                    weights(w1, 1, 1, UNIT)
            sp.dma_start(ident[:], eye).then_inc(ident_in, 16)
            sp.dma_start(onehot_sb[:], onehot).then_inc(onehot_in, 16)
            sp.dma_start(rel_sb[0:BUCKETS, :], rel).then_inc(rel_in, 16)
            sp.dma_start(ws_sb[:], wsT).then_inc(ws_in, 16)
            sp.dma_start(ln_sb[:], lnrow.partition_broadcast(P)).then_inc(mix_in, 16)
            sp.wait_ge(dw_zero, 1)
            for g in range(4):
                rows = slice(64 * (g % 2), 64 * (g % 2) + 64)
                sp.dma_start(dw_sb[rows, g // 2, rows], dw[g]).then_inc(mix_in, 16)
                sp.dma_start(bs_sb[rows, g // 2, :], bsrow[g].partition_broadcast(64)).then_inc(mix_in, 16)

            for u_ in range(2, U_GATE):
                weights(w1, u_, u_, UNIT)
            for i in range(N_GATE):
                weights(w2, i, U_GATE + i, GUNIT)
            for i in range(N_UNITS - U_WO):
                weights(w3, i, U_WO + i, UNIT)
            done = {OUT_DVE: 0, OUT_POOL: 0}
            for h, m in OUT_SENT:
                by, scaled = (OUT_DVE, out_dve) if m in OUT_DVE[h] else (OUT_POOL, out_pool)
                done[by] += 1
                sp.wait_ge(scaled, done[by])
                sp.dma_start(out[m * P:(m + 1) * P, hs_(h)], M[:, m, hs_(h)]).then_inc(out_sent, 16)
            sp.wait_ge(out_sent, 16 * KT * NH)

        @block.gpsimd
        def _(pool):
            def unit_used(u):
                if u < U_TM:
                    pool.wait_ge(half_done, 2 * u + 2)
                elif u < U_QK1:
                    part, i = divmod(u - U_TM, 4)
                    if i < 3:
                        pool.wait_ge(w_used, 3 * part + i + 1)
                    else:
                        pool.wait_ge(tmB_done if part else tmA_done, TT)
                elif u < U_GATE:
                    pool.wait_ge(half_done, H_QK1 + 2 * (u - U_QK1) + 2)
                elif u < U_WO:
                    pool.wait_ge(y_ps, 2 * (u - U_GATE) + 2)
                else:
                    pool.wait_ge(half_done, H_WO + 2 * (u - U_WO) + 2)

            def split(u, n):
                pool.wait_ge(w_in[u % 2], 16 * (u // 2 + 1))
                if u >= 2:
                    unit_used(u - 2)
                raw, hi, lo = WR[:, u % 2, 0:n], WH[:, u % 2, 0:n], WL[:, u % 2, 0:n]
                pool.tensor_tensor(hi, raw, ones[:, 0:1].to_broadcast([P, n]), ALU.mult).then_inc(w_hi_done, 1)
                pool.wait_ge(w_hi_done, u + 1)
                pool.tensor_tensor(lo, raw, hi.bitcast(F32), ALU.subtract).then_inc(w_split, 1)

            pool.wait_ge(ones_set, 1)
            def square_x(k):
                pool.wait_ge(x_in[k], 16)
                pool.tensor_tensor(sqp[:, k, :], xs[:, k, :], xs[:, k, :], ALU.mult).then_inc(pool_sq_part, 1)

            square_x(0)
            pool.wait_ge(w_split, 1)
            split(1, UNIT)
            square_x(1)
            pool.wait_ge(pool_sq_part, 2)
            pool.tensor_tensor(sqp[:, 0, :], sqp[:, 0, :], sqp[:, 1, :], ALU.add).then_inc(pool_sq, 1)
            pool.wait_ge(ws_in, 16)
            pool.affine_select(out=ws_sb[:], in_=ws_sb[:], compare_op=ALU.is_ge, fill=0.0, base=0,
                               pattern=[[0, 4], [1, P]], channel_multiplier=-1).then_inc(ws_masked, 1)
            for u_ in range(2, N_UNITS):
                split(u_, GUNIT if U_GATE <= u_ < U_WO else UNIT)
                if u_ == U_WO:
                    for k in POOL_LOWS:
                        pool.wait_ge(m_hi, k + 1)
                        h0 = hs_(0)
                        pool.tensor_tensor(H[:, 1, k, h0], M[:, k, h0], H[:, 0, k, h0].bitcast(F32), ALU.subtract).then_inc(m_lo_pool, 1)
            for h in range(NH):
                pool.wait_ge(rsb_set, 3 + h)
                for m in OUT_POOL[h]:
                    pool.wait_ge(x3_g, 2 * m + h + 1)
                    pool.tensor_tensor(M[:, m, hs_(h)], M[:, m, hs_(h)], rs_b[:, hs_(h)], ALU.mult).then_inc(out_pool, 1)

        @block.tensor
        def _(pe):
            def split_mm(bank, w, slot, wcol, acts, ak, sl, first, last):
                wh, wl = WH[:, slot, wcol:wcol + P], WL[:, slot, wcol:wcol + P]
                pe.matmul(bank, wh, acts[:, 0, ak, sl], start=first, stop=False)
                pe.matmul(bank, wh, acts[:, 1, ak, sl], start=False, stop=False)
                return pe.matmul(bank, wl, acts[:, 0, ak, sl], start=False, stop=last)

            def unit(u, hs, acts, before=None, at={}):
                pe.wait_ge(w_split, u + 1)
                for h in range(NH):
                    if hs >= H_QK1:
                        pe.wait_ge(half_free, hs + h - 3)
                    elif hs >= 6:
                        pe.wait_ge(half_free, hs + h - 5)
                    for k in range(KT):
                        if before:
                            before(k, h)
                        if (k, h) in at:
                            at[k, h]()
                        mm = split_mm(bank_of(hs + h), WH, u % 2, k * P, acts, k, hs_(h), k == 0, k == KT - 1)
                    mm.then_inc(half_done, 1)

            def column_sums(bank, ready, n, tiles):
                pe.wait_ge(ready, n)
                for c, toks in enumerate(tiles):
                    mm = pe.matmul(bank[:, c:c + 1], sqacc[:, toks], ones[:, 0:1], start=True, stop=True)
                mm.then_inc(ssq_ps, 1)

            def spread(h, n, slot):
                pe.wait_ge(diag_ready, n)
                for part in range(2):
                    mm = pe.matmul(ps[6 + h][:], ones_r[:], diag[:, slot + part, :], start=not part, stop=bool(part))
                mm.then_inc(rsb_ps, 1)

            plain = [slice(t * P, (t + 1) * P) for t in range(TT)]

            pe.wait_ge(w_split, 1)
            for u_, k in ((0, 0), (0, 1), (0, 2), (0, 3), (1, 0), (1, 1), (0, 4), (1, 2), (0, 5), (1, 3), (0, 6), (1, 4),
                          (0, 7), (1, 5), (1, 6), (1, 7)):
                if u_ == 0:
                    pe.wait_ge(h_hi, k + 1)
                    for h in range(NH):
                        for w in (WH, WL):
                            pe.matmul(bank_of(h), w[:, 0, k * P:(k + 1) * P], H[:, 0, k, hs_(h)], start=k == 0 and w is WH, stop=False)
                    pe.wait_ge(h_lo, k + 1)
                    for h in range(NH):
                        mm = pe.matmul(bank_of(h), WH[:, 0, k * P:(k + 1) * P], H[:, 1, k, hs_(h)], start=False, stop=k == KT - 1)
                        if k == KT - 1:
                            mm.then_inc(half_done, 1)
                    continue
                if k == 0:
                    pe.wait_ge(w_split, 2)
                for h in range(NH):
                    mm = split_mm(bank_of(2 + h), WH, 1, k * P, H, k, hs_(h), k == 0, k == KT - 1)
                    if k == KT - 1:
                        mm.then_inc(half_done, 1)
            pe.wait_ge(ones_set, 2)
            unit(2, 4, H, at={
                (0, 0): lambda: column_sums(ps[6], sq_used, KT - 1, plain + [strided(t) for t in range(TT)]),
                (1, 1): lambda: spread(0, 1, 0), (3, 1): lambda: spread(1, 2, 2)})
            pe.wait_ge(rsb_set, 1)
            pe.wait_ge(onehot_in, 16)
            pe.wait_ge(rel_set, 1)
            pe.wait_ge(rel_in, 16)

            def distances(g):
                pe.matmul(ps[6 + g % 2][0:HEADS, 0:DIST], rel_sb[:, g * HEADS:(g + 1) * HEADS],
                          onehot_sb[:, g, :], start=True, stop=True).then_inc(dist_ps, 1)

            distances(0)
            distances(1)
            unit(3, 6, H)
            pe.wait_ge(dist_set, 1)
            distances(2)
            unit(4, 8, H)
            unit(5, 10, H)

            for part in range(2):
                for i in range(4):
                    u_ = U_TM + 4 * part + i
                    pe.wait_ge(w_split, u_ + 1)
                    for t in range(TT):
                        if i == 0 and part == 0:
                            if t < 6:
                                pe.wait_ge(half_free, 7 + t)
                            else:
                                pe.wait_ge(dist_set, 2 if t == 7 else 3)
                        if i == 0 and part == 1:
                            pe.wait_ge(tm_dve if t % 2 else tm_act, t // 2 + 1)
                        toks = slice(t * P, (t + 1) * P) if part == 0 else strided(t)
                        for kk in range(2):
                            k = 2 * i + kk
                            hi, lo = H[:, 0, k, toks], H[:, 1, k, toks]
                            wh, wl = (w[:, u_ % 2, kk * HALF:(kk + 1) * HALF] for w in (WH, WL))
                            pe.matmul(ps[t][:], hi, wh, start=(k == 0), stop=False)
                            pe.matmul(ps[t][:], hi, wl, start=False, stop=False)
                            mm = pe.matmul(ps[t][:], lo, wh, start=False, stop=(k == KT - 1))
                        if i == 3:
                            mm.then_inc(tmB_done if part else tmA_done, 1)
                    if i < 3:
                        mm.then_inc(w_used, 1)

            def attention(pair):
                jobs = jobs_of(pair)
                base = len(jobs) * pair

                def scores(i):
                    n, (hh, part, t) = base + i, jobs[i]
                    if n >= 4:
                        pe.wait_ge(m_ready, n - 3)
                    rows = slice(64 * hh, 64 * hh + DH)
                    bank = ps[S_BANKS[n % 4]]
                    if part == 0:
                        ks = slice(max(t - 1, 0) * P, (t + 1) * P)
                        W = P if t == 0 else 2 * P
                        mm = pe.matmul(bank[:, 0:W], qk[rows, 0, t * P:(t + 1) * P], qk[rows, 1, ks], start=True, stop=True)
                    else:
                        blk, r = divmod(t, 4)
                        W = P * (blk + 1)
                        for g in range(2):
                            mm = pe.matmul(bank[:, g * W:(g + 1) * W], qk[rows, 2 + 2 * g, strided(t)],
                                           qk[rows, 3 + 2 * g, r:(blk + 1) * HALF:4], start=True, stop=True)
                    mm.then_inc(s_ready, 1)

                def turn(i):
                    n, (hh, part, t) = base + i, jobs[i]
                    pe.wait_ge(p_ready, n + 1)
                    if n >= 2:
                        pe.wait_ge(t_free, n - 1)
                    for c in range(len(key_tiles(part, t))):
                        mm = pe.transpose(ps[6 + n % 2][:, c * P:(c + 1) * P], T[:, n % 4, c * P:(c + 1) * P], ident[:])
                    mm.then_inc(t_ready, 1)

                def weighted(i):
                    n, (hh, part, t) = base + i, jobs[i]
                    pe.wait_ge(t_free, n + 1)
                    if n >= 2:
                        pe.wait_ge(o_free, n - 1)
                    head = 2 * pair + hh
                    kts = key_tiles(part, t)
                    for c, (g, kt) in enumerate(kts):
                        v = va0[:, kt, WIDTH + head * DH:WIDTH + (head + 1) * DH] if part == 0 else \
                            v12[:, kt, g * WIDTH + head * DH:g * WIDTH + (head + 1) * DH]
                        mm = pe.matmul(ps[n % 2][64 * hh:64 * hh + DH, 0:P], v, pts[:, n % 2, c * P:(c + 1) * P],
                                       start=(c == 0), stop=(c == len(kts) - 1))
                    mm.then_inc(pv_done, 1)

                def step(i):
                    if i < len(jobs):
                        scores(i)
                    if 0 <= i - 3 < len(jobs):
                        turn(i - 3)
                    if 0 <= i - 4 < len(jobs):
                        weighted(i - 4)

                for i in range(len(jobs)):
                    step(i)
                return {(k, 0): lambda i=i: step(len(jobs) + i) for i, k in enumerate((1, 3, 5, 7))}

            pe.wait_ge(tm_dve, TT)
            pe.wait_ge(tm_act, TT)
            pe.wait_ge(half_free, 2 * N_QK)
            rest = attention(0)
            pe.wait_ge(m_ready, 30)
            unit(U_QK1, H_QK1, H, at=rest)
            pe.wait_ge(o_free, 32)
            for i in range(1, N_QK):
                unit(U_QK1 + i, H_QK1 + 2 * i, H)
            pe.wait_ge(half_free, H_MIX)
            rest = attention(1)
            pe.wait_ge(m_ready, 62)
            unit(U_MIX, H_MIX, H, at=rest)
            pe.wait_ge(o_free, 64)
            pe.wait_ge(t_free, 64)
            pe.transpose(ps[7][:, 0:P], stats[:], ident[:]).then_inc(statsT_ps, 1)
            unit(U_MIX + 1, H_MIX + 2, H)
            unit(U_MIX + 2, H_MIX + 4, H)
            pe.wait_ge(v_ready, 1)
            pe.wait_ge(mix_in, 16 * MIX_DMAS)
            pe.wait_ge(ws_masked, 1)
            pe.wait_ge(rowsT_set, 1)
            for pr in range(BT):
                for h in range(NH):
                    for c in range(4):
                        for gg in range(2):
                            g = 2 * pr + gg
                            mm = pe.matmul(ps[4 + 2 * pr + h][64 * gg:64 * gg + 64, c * P:(c + 1) * P],
                                           va0[:, 4 * h + c, g * 64:(g + 1) * 64], ws_sb[:, g, :], start=True, stop=True)
                    mm.then_inc(sv_done, 1)
            for i in range(3, 8):
                unit(U_MIX + i, H_MIX + 2 * i, H)
            pe.wait_ge(pool_ready, 1)
            pe.wait_ge(sv_free, 4)
            for tile in range(BT):
                for h in range(NH):
                    pe.matmul(ps[4 + 2 * tile + h][:], dw_sb[:, tile, :], z[:, tile, hs_(h)],
                              start=True, stop=True).then_inc(dmm_done, 1)
            for i in range(8, N_MIX):
                unit(U_MIX + i, H_MIX + 2 * i, H)

            for j in range(KT):
                for b, pos in enumerate(GATE_ORDER):
                    i = 4 * j + b
                    u_, hs = U_GATE + i, H_GATE + 2 * i
                    pe.wait_ge(w_split, u_ + 1)
                    for h in range(NH):
                        n = 2 * i + h
                        pe.wait_ge(half_free, hs + h - 3)
                        for k in range(KT):
                            mm = split_mm(bank_of(hs + h), WH, u_ % 2, k * P, H, k, hs_(h), k == 0, k == KT - 1)
                        mm.then_inc(half_done, 1)
                        if n == 0:
                            pe.wait_ge(y_lo[POS_D], 4)
                        if j == 0:
                            pe.wait_ge(y_lo[pos], 2 if pos == POS_C else 4)
                        if n >= 2:
                            pe.wait_ge(y_free, n - 1)
                        for k in range(BT):
                            mm = split_mm(ps[4 + n % 2][:], WH, u_ % 2, UNIT + k * P, Y, 2 * pos + k, hs_(h), k == 0, k == BT - 1)
                        mm.then_inc(y_ps, 1)

            def merged_split(k, h):
                if (h, k) in DVE_LOWS:
                    pe.wait_ge(m_lo, DVE_LOWS.index((h, k)) + 1)
                else:
                    pe.wait_ge(m_lo_pool, POOL_LOWS.index(k) + 1)

            for j in range(KT):
                unit(U_WO + j, H_WO + 2 * j, H,
                     merged_split if j == 0 else None)

            for c in range(CHUNKS):
                u_, hs = U_FF + 2 * KT * c, H_FF + 4 * KT * c
                for m in range(KT):
                    at = {}
                    if c == 0 and m == 0:
                        at = {(0, 1): lambda: column_sums(ps[6], x2_sum, 2 * KT, plain),
                              (5, 1): lambda: spread(0, 3, 0), (7, 1): lambda: spread(1, 4, 2)}
                    unit(u_ + m, hs + 2 * m, Y,
                         (lambda k, h: pe.wait_ge(xg_lo, 2 * k + h + 1)) if c == 0 and m == 0 else None,
                         at)
                for m in range(KT):
                    at = {}
                    if c == CHUNKS - 1 and m == KT - 1:
                        at = {(3, 1): lambda: column_sums(ps[6], x3_sum, 2 * KT - 1, plain[:TT // 2]), (7, 1): lambda: spread(0, 5, 2)}
                    unit(u_ + KT + m, hs + 2 * KT + 2 * m, H,
                         (lambda k, h: pe.wait_ge(f_lo, 2 * KT * c + 2 * k + h + 1)) if m == 0 else None, at)
            column_sums(ps[7], x3_sum, 2 * KT, plain[TT // 2:])
            spread(1, 6, 0)

        @block.vector
        def _(dve):
            chain = [0]

            def link(ins):
                chain[0] += 1
                ins.then_inc(dve_chain, 1)
                dve.wait_ge(dve_chain, chain[0])

            def factor_columns(n, sums, cols):
                dve.wait_ge(ssq_ps, n + 1)
                dve.tensor_scalar(vcol[:, 1, cols], sums, 1.0 / D, EPS, ALU.mult, ALU.add).then_inc(var_ready, 1)
                dve.wait_ge(var_ready, n + 1)
                dve.wait_ge(std_ready, n + 1)
                inv_newton(cols, rs_col[:, cols])
                link(dve.tensor_copy(rs_hi[:, cols], rs_col[:, cols]))
                link(dve.tensor_tensor(rs_lo[:, cols], rs_col[:, cols], rs_hi[:, cols].bitcast(F32), ALU.subtract))

            def diagonals(h, slot):
                nb = TT // NH
                for part, src in enumerate((rs_hi, rs_lo)):
                    last = dve.tensor_tensor(diag[:, slot + part, :].rearrange("p (c k) -> p c k", c=nb),
                                             ident[:].unsqueeze(1).to_broadcast([P, nb, P]),
                                             src[:, nb * h:nb * (h + 1)].bitcast(F32).unsqueeze(2).to_broadcast([P, nb, P]), ALU.mult)
                last.then_inc(diag_ready, 1)

            def norm_factor(n):
                cols = 2 * TT if n == 0 else TT
                dve.wait_ge(ident_in, 16)
                factor_columns(n, ps[6][:, 0:cols], slice(0, cols))
                for h in range(NH):
                    diagonals(h, 2 * h)
                for h in range(NH):
                    dve.wait_ge(rsb_ps, 2 * n + h + 1)
                    last = dve.tensor_copy(rs_b[:, hs_(h)], ps[6 + h][:])
                last.then_inc(rsb_set, 1)
                dve.wait_ge(rsb_set, n + 1)

            def inv_newton(cols, res):
                var, root, inv, tmp = (vcol[:, i, cols] for i in range(1, 5))
                link(dve.reciprocal(inv, root))
                link(dve.tensor_tensor(tmp, inv, inv, ALU.mult))
                link(dve.tensor_tensor(tmp, tmp, var, ALU.mult))
                link(dve.tensor_scalar(tmp, tmp, -0.5, 1.5, ALU.mult, ALU.add))
                link(dve.tensor_tensor(res, inv, tmp, ALU.mult))

            def take(hs, dst):
                dve.wait_ge(half_done, hs + 1)
                h = hs % 2
                return dve.tensor_tensor(dst, bank_of(hs), rs_b[:, hs_(h)], ALU.mult).then_inc(half_free, 1)

            dve.memset(ones[:], 1.0).then_inc(ones_set, 1)
            dve.wait_ge(ones_set, 1)
            dve.tensor_copy(ones_r[:], ones[:, 0:1].to_broadcast([P, P])).then_inc(ones_set, 1)
            dve.memset(rel_sb[BUCKETS:BUCKETS + 1, :], NEG).then_inc(rel_set, 1)
            dve.memset(dw_sb[:], 0.0).then_inc(dw_zero, 1)

            dve.wait_ge(w_hi_done, 1)
            dve.tensor_tensor(WL[:, 0, 0:UNIT], WR[:, 0, 0:UNIT], WH[:, 0, 0:UNIT].bitcast(F32), ALU.subtract).then_inc(w_split, 1)
            dve.wait_ge(tab_in, 16)
            def sum_sq(k):
                dve.wait_ge(sq_ready, k - 1)
                if k == 2:
                    dve.tensor_copy(sqacc[:], sq[:, 0, :]).then_inc(sq_used, 1)
                else:
                    dve.wait_ge(sq_used, k - 2)
                    dve.tensor_tensor(sqacc[:], sqacc[:], sq[:, k % 2, :], ALU.add).then_inc(sq_used, 1)

            for k in range(KT):
                dve.wait_ge(h_hi, k + 1)
                dve.scalar_tensor_tensor(out=H[:, 1, k, :], in0=xs[:, k, :], scalar=cl[:, C_GMIX + k:C_GMIX + k + 1],
                                         in1=H[:, 0, k, :].bitcast(F32), op0=ALU.mult, op1=ALU.subtract).then_inc(h_lo, 1)
                if k >= 3:
                    sum_sq(k - 1)
            sum_sq(KT - 1)
            dve.wait_ge(pool_sq, 1)
            dve.wait_ge(sq_used, KT - 2)
            dve.tensor_tensor(sqacc[:], sqacc[:], sqp[:, 0, :], ALU.add).then_inc(sq_used, 1)
            norm_factor(0)
            for hs in range(2 * N_QK):
                take(hs, qk[:, hs // 2, hs_(hs % 2)])
                for g in {3: (0, 1), 7: (2,)}.get(hs, ()):
                    dve.wait_ge(dist_ps, g + 1)
                    dve.tensor_scalar(dist_sb[:, g, :], ps[6 + g % 2][0:HEADS, 0:DIST], DH ** 0.5, None, ALU.mult).then_inc(dist_set, 1)
            dve.wait_ge(dist_out, 48)
            for part in range(2):
                for t in range(1, TT, 2):
                    dve.wait_ge(tmB_done if part else tmA_done, t + 1)
                    dve.tensor_scalar((v12 if part else va0)[:, t, :], ps[t][:], rs_col[:, part * TT + t:part * TT + t + 1], None,
                                      ALU.mult).then_inc(tm_dve, 1)

            def attention(pair):
                jobs = jobs_of(pair)
                base = len(jobs) * pair
                for i in range(len(jobs) + 5):
                    if i < len(jobs):
                        n, (hh, part, t) = base + i, jobs[i]
                        head = 2 * pair + hh
                        W = P * len(key_tiles(part, t))
                        dve.wait_ge(s_ready, n + 1)
                        if n >= 4:
                            dve.wait_ge(t_ready, n - 3)
                        if part == 0:
                            b_ap = bias[:, head, 0, WIDTH - W:WIDTH]
                            o_ap, s_ap = T[:, n % 4, 0:W], ps[S_BANKS[n % 4]][:, 0:W]
                        else:
                            b_ap = bias[:, head, 1:3, WIDTH - W // 2:WIDTH]
                            o_ap, s_ap = (a.rearrange("p (g k) -> p g k", g=2) for a in (T[:, n % 4, 0:W], ps[S_BANKS[n % 4]][:, 0:W]))
                        col = part * 32 + head * TT + t
                        dve.tensor_tensor_reduce(out=o_ap, in0=s_ap, in1=b_ap, scale=-DH ** -0.5, scalar=-NEG, op0=ALU.add,
                                                 op1=ALU.min, accum_out=stats[:, col:col + 1]).then_inc(m_ready, 1)
                    if 0 <= i - 5 < len(jobs):
                        n, (hh, part, t) = base + i - 5, jobs[i - 5]
                        rows = slice(64 * hh, 64 * hh + DH)
                        toks = slice(t * P, (t + 1) * P) if part == 0 else strided(t)
                        dve.wait_ge(pv_done, n + 1)
                        dve.tensor_copy(O[rows, part, pair, toks], ps[n % 2][rows, 0:P]).then_inc(o_free, 1)

            dve.wait_ge(bias_in, 48)
            attention(0)
            def gelu2(n, x):
                r = T[:, n % 4, :]
                if len(x.shape) == 3:
                    r = r.rearrange("p (a b) -> p a b", a=x.shape[1])
                dve.wait_ge(g_sq, n + 1)
                link(dve.tensor_scalar(r, r, GELU_A, 1.0, ALU.mult, ALU.add))
                dve.tensor_tensor(r, r, x, ALU.mult).then_inc(g_in, 1)
                dve.wait_ge(g_th, n + 1)
                link(dve.scalar_tensor_tensor(out=x, in0=r, scalar=1.0, in1=x, op0=ALU.add, op1=ALU.mult))

            def gelu_v(n):
                a = 2 * n
                gelu2(n, va0[:, a:a + 2, 0:WIDTH])

            for i in range(4):
                take(H_QK1 + i, qk[:, i // 2, hs_(i % 2)])
                gelu_v(i)
            for t in range(TT):
                link(dve.bn_stats(small[:, t, 0:6], va0[:, t, 0:WIDTH]))
                last = dve.bn_aggr(small[:, t, 6:8], small[:, t, 0:6])
            link(last)
            dve.tensor_scalar(vcol[:, 1, 0:TT], small[:, :, 7], 0.25, EPS, ALU.mult, ALU.add).then_inc(ln_var, 1)
            dve.wait_ge(ln_var, 1)
            dve.wait_ge(ln_std, 1)
            tt = slice(0, TT)
            inv_newton(tt, vcol[:, 0, tt])
            link(dve.tensor_scalar(vcol[:, 0, tt], vcol[:, 0, tt], 0.5, None, ALU.mult))

            def normed(t):
                v = va0[:, t, 0:WIDTH]
                link(dve.tensor_scalar(v, v, small[:, t, 6:7], vcol[:, 0, t:t + 1], ALU.subtract, ALU.mult))
                link(dve.tensor_tensor(v, v, ln_sb[:, 0, :], ALU.mult))
                return dve.tensor_tensor(v, v, ln_sb[:, 1, :], ALU.add)

            dve.wait_ge(mix_in, 16 * MIX_DMAS)
            for i in range(4, 2 * N_QK):
                take(H_QK1 + i, qk[:, i // 2, hs_(i % 2)])
                last = normed(i - 4)
            last.then_inc(v_ready, 1)
            attention(1)

            def gelu_u(i):
                take(H_MIX + i, u[:, i // 2, hs_(i % 2)])
                dve.wait_ge(half_free, H_MIX + i + 1)
                gelu2(4 + i, u[:, i // 2, hs_(i % 2)])

            gelu_u(0)
            gelu_u(1)
            dve.wait_ge(statsT_ps, 1)
            dve.tensor_copy(rowsT[:], ps[7][:, 0:P]).then_inc(rowsT_set, 1)
            gelu_u(2)
            gelu_u(3)

            def piece(q):
                return q // 2, hs_(q % 2)

            for q in range(4):
                dve.wait_ge(sv_done, q + 1)
                r = T[:, q, :].rearrange("p (c t) -> p c t", c=4)
                dve.tensor_tensor(r, ps[4 + q][:].rearrange("p (c t) -> p c t", c=4),
                                  bs_sb[:, q // 2, :].unsqueeze(1).to_broadcast([P, 4, P]), ALU.add).then_inc(sv_free, 1)
                dve.wait_ge(sv_free, q + 1)
                x = u[:, q // 2, hs_(q % 2)]
                dve.tensor_tensor(x, x, T[:, q, :], ALU.mult).then_inc(y_val[POS_A], 1)

            def doubled(dst, src, back, rows):
                d, s = dst[rows, :], src[rows, :]
                dve.tensor_copy(d[:, 0:back], s[:, 0:back])
                link(dve.tensor_tensor(d[:, back:S], s[:, back:S], s[:, 0:S - back], ALU.add))

            sB, all_rows, lower, upper = sqacc, slice(0, P), slice(0, 64), slice(64, P)

            def pooled(tile):
                doubled(sA, z[:, tile, :], 1, all_rows)
                if tile == 0:
                    doubled(sB, sA, 2, upper)
                else:
                    doubled(sB, sA, 2, all_rows)
                    doubled(sA, sB, 4, all_rows)
                    doubled(sB, sA, 8, upper)
                ratio = cl[:, C_RATIO + 16 * tile:C_RATIO + 16 * (tile + 1)]
                for rows, sums in ((lower, sA), (upper, sB)):
                    s = sums[rows, :]
                    link(dve.tensor_tensor(s[:, 0:16], s[:, 0:16], ratio[rows, :], ALU.mult))
                    last = dve.scalar_tensor_tensor(out=z[rows, tile, :], in0=s, scalar=cl[rows, C_WINV + tile:C_WINV + tile + 1],
                                                    in1=z[rows, tile, :], op0=ALU.mult, op1=ALU.subtract)
                return last

            take(H_MIX + 4, zz(0))
            take(H_MIX + 5, zz(1))
            dve.wait_ge(half_free, H_MIX + 6)
            link(pooled(0))

            dve.wait_ge(rows_in, 16)
            nat = lambda a: a.rearrange("h (p r) -> h p r", r=4)
            per = lambda a: a.rearrange("h (r p) -> h p r", r=4)
            neg0, neg1, den0, den1 = nat(R[:, 0, :]), per(R[:, 1, :]), nat(R[:, 2, :]), per(R[:, 3, :])
            e0, e1, t0, t1, inv = nat(R[:, 0, :]), nat(rt[:, 1, :]), nat(rt[:, 0, :]), nat(R[:, 1, :]), nat(R[:, 2, :])
            link(dve.tensor_tensor(t0, neg0, neg1, ALU.min))
            link(dve.tensor_tensor(e1, t0, neg1, ALU.subtract))
            dve.tensor_tensor(e0, t0, neg0, ALU.subtract).then_inc(rexp_in, 1)
            dve.wait_ge(rexp_out, 2)
            dve.tensor_tensor(t0, e0, den0, ALU.mult)
            link(dve.tensor_tensor(t1, e1, den1, ALU.mult))
            link(dve.tensor_tensor(t0, t0, t1, ALU.add))
            link(dve.reciprocal(R[:, 2, :], rt[:, 0, :]))
            dve.tensor_tensor(e0, e0, inv, ALU.mult)
            dve.tensor_tensor(e1, e1, inv, ALU.mult).then_inc(mixw_set, 1)

            take(H_MIX + 6, zz(2))
            take(H_MIX + 7, zz(3))
            dve.wait_ge(half_free, H_MIX + 8)
            pooled(1).then_inc(pool_ready, 1)

            for i in range(8, 12):
                take(H_MIX + i, tc[:, (i - 8) // 2, hs_(i % 2)])

            def low(pos, n, val, dst, scale=1.0):
                dve.wait_ge(y_hi[pos], n + 1)
                dve.scalar_tensor_tensor(out=Y[:, 1, 2 * pos + dst[0], dst[1]], in0=val, scalar=scale,
                                         in1=Y[:, 0, 2 * pos + dst[0], dst[1]].bitcast(F32),
                                         op0=ALU.mult, op1=ALU.subtract).then_inc(y_lo[pos], 1)

            def attn_mix(pr):
                a, b = O[:, 0, pr, :], O[:, 1, pr, :]
                dve.tensor_tensor(a, a, wb[:, 0, pr, :], ALU.mult)
                link(dve.tensor_tensor(b, b, wb[:, 1, pr, :], ALU.mult))
                dve.tensor_tensor(a, a, b, ALU.add).then_inc(y_val[POS_C], 1)

            def conv(tile):
                c, x = cv[:, tile, :], tc[:, tile, :]
                w = [cl[:, C_CONV + 2 * j + tile:C_CONV + 2 * j + tile + 1] for j in range(3)]
                link(dve.tensor_scalar(c, x, w[2], None, ALU.mult))
                for back in (1, 2):
                    link(dve.scalar_tensor_tensor(out=c[:, back:S], in0=x[:, 0:S - back], scalar=w[2 - back],
                                                  in1=c[:, back:S], op0=ALU.mult, op1=ALU.add))

            def conv_in(i):
                take(H_MIX + i, T[:, i % 4, :])
                dve.wait_ge(half_free, H_MIX + i + 1)
                x = tc[:, (i - 12) // 2, hs_(i % 2)]
                return dve.tensor_tensor(x, x, T[:, i % 4, :], ALU.mult)

            dve.wait_ge(wb_in, 16 * 8)
            attn_mix(0)
            attn_mix(1)
            dve.wait_ge(y_val[POS_C], 2)
            for tile in range(BT):
                conv_in(12 + 2 * tile)
                link(conv_in(13 + 2 * tile))
                conv(tile)
            for q in range(4):
                low(POS_A, q, u[:, q // 2, hs_(q % 2)], piece(q), 0.5)
            dve.wait_ge(dmm_done, 4)
            for q in range(4):
                low(POS_D, q, ps[4 + q][:], piece(q), cl[:, C_DSC + q // 2:C_DSC + q // 2 + 1])
            for pr in range(BT):
                low(POS_C, pr, O[:, 0, pr, :], (pr, slice(0, S)))
            for q in range(5):
                if q < 4:
                    take(H_MIX + 16 + q, T[:, q, :])
                    dve.wait_ge(half_free, H_MIX + 16 + q + 1)
                    x = cv[:, q // 2, hs_(q % 2)]
                    dve.tensor_tensor(x, x, T[:, q, :], ALU.mult).then_inc(y_val[POS_B], 1)
                if q >= 1:
                    low(POS_B, q - 1, cv[:, (q - 1) // 2, hs_((q - 1) % 2)], piece(q - 1))

            def gate_terms(n):
                j, b, h = n // 8, n // 2 % 4, n % 2
                dve.wait_ge(tanh_done, n + 1)
                dve.wait_ge(y_ps, n + 1)
                r, m = T[:, n % 4, :], M[:, j, hs_(h)]
                ins = dve.scalar_tensor_tensor(out=m if b == 0 else r, in0=r, scalar=1.0, in1=ps[4 + n % 2][:],
                                               op0=ALU.add, op1=ALU.mult).then_inc(y_free, 1)
                if b:
                    dve.wait_ge(y_free, n + 1)
                    ins = dve.tensor_tensor(m, m, r, ALU.add)
                if b == 3:
                    ins.then_inc(m_set, 1)

            for n in range(2 * N_GATE):
                take(H_GATE + n, T[:, n % 4, :])
                if 1 <= n < 2 * N_GATE - 1:
                    gate_terms(n - 1)
            for i, (h, k) in enumerate(DVE_LOWS):
                if i == 2:
                    gate_terms(2 * N_GATE - 2)
                if i == 3:
                    gate_terms(2 * N_GATE - 1)
                dve.wait_ge(m_hi, KT * h + k + 1)
                dve.tensor_tensor(H[:, 1, k, hs_(h)], M[:, k, hs_(h)], H[:, 0, k, hs_(h)].bitcast(F32), ALU.subtract).then_inc(m_lo, 1)

            def acc_sq(n, ready, done):
                dve.wait_ge(ready, n + 1)
                a = sqacc[:, hs_(n % 2)]
                if n < 2:
                    dve.tensor_copy(a, T[:, n % 2, :]).then_inc(done, 1)
                else:
                    dve.wait_ge(done, n - 1)
                    dve.tensor_tensor(a, a, T[:, n % 2, :], ALU.add).then_inc(done, 1)

            for n in range(2 * KT + 1):
                if n < 2 * KT:
                    j, h = n // 2, n % 2
                    dve.wait_ge(xr_in[n % 2], 16 * (n // 2 + 1))
                    dve.wait_ge(half_done, H_WO + n + 1)
                    dve.scalar_tensor_tensor(out=M[:, j, hs_(h)], in0=bank_of(H_WO + n), scalar=0.5, in1=T[:, 2 + n % 2, :],
                                             op0=ALU.mult, op1=ALU.add).then_inc(half_free, 1)
                if n >= 1:
                    j, h = (n - 1) // 2, (n - 1) % 2
                    dve.wait_ge(xg_hi, n)
                    dve.scalar_tensor_tensor(out=Y[:, 1, j, hs_(h)], in0=M[:, j, hs_(h)], scalar=cl[:, C_GFF + j:C_GFF + j + 1],
                                             in1=Y[:, 0, j, hs_(h)].bitcast(F32), op0=ALU.mult, op1=ALU.subtract).then_inc(xg_lo, 1)
                    acc_sq(n - 1, x2_sq, x2_sum)
            norm_factor(1)

            def final_scale(h, tiles):
                dve.wait_ge(rsb_set, 3 + h)
                for m in tiles:
                    dve.wait_ge(x3_g, 2 * m + h + 1)
                    dve.tensor_tensor(M[:, m, hs_(h)], M[:, m, hs_(h)], rs_b[:, hs_(h)], ALU.mult).then_inc(out_dve, 1)

            for c in range(CHUNKS):
                for n in range(2 * KT + 1):
                    if n < 2 * KT:
                        hs = H_FF + 4 * KT * c + n
                        dve.wait_ge(half_done, hs + 1)
                        dve.scalar_tensor_tensor(out=T[:, n % 4, :], in0=bank_of(hs), scalar=0.0, in1=rs_b[:, hs_(n % 2)],
                                                 op0=ALU.max, op1=ALU.mult).then_inc(half_free, 1)
                    if n >= 1:
                        m, h = (n - 1) // 2, (n - 1) % 2
                        dve.wait_ge(f_hi, 2 * KT * c + n)
                        dve.tensor_tensor(H[:, 1, m, hs_(h)], T[:, (n - 1) % 4, :], H[:, 0, m, hs_(h)].bitcast(F32),
                                          ALU.subtract).then_inc(f_lo, 1)
                for n in range(2 * KT):
                    hs = H_FF + 4 * KT * c + 2 * KT + n
                    m = M[:, n // 2, hs_(n % 2)]
                    dve.wait_ge(half_done, hs + 1)
                    dve.tensor_tensor(m, m, bank_of(hs), ALU.add).then_inc(half_free, 1)
                    if c == CHUNKS - 1:
                        if 1 <= n <= 2 * KT - 2:
                            acc_sq(n - 1, x3_sq, x3_sum)
                        if n == 2 * KT - 2:
                            acc_sq(n, x3_sq, x3_sum)
                            factor_columns(2, ps[6][:, 0:4], slice(0, 4))
                            diagonals(0, 2)
            final_scale(0, OUT_DVE[0][:1])
            acc_sq(2 * KT - 1, x3_sq, x3_sum)
            final_scale(0, OUT_DVE[0][1:2])
            factor_columns(3, ps[7][:, 0:4], slice(4, 8))
            diagonals(1, 0)
            final_scale(0, OUT_DVE[0][2:])
            final_scale(1, OUT_DVE[1])

        @block.scalar
        def _(act):
            chain = [0]

            def link(ins):
                chain[0] += 1
                ins.then_inc(act_chain, 1)
                act.wait_ge(act_chain, chain[0])

            def root(n, cols, ready, done):
                act.wait_ge(ready, n + 1)
                act.activation(vcol[:, 2, cols], vcol[:, 1, cols], ACT.Sqrt).then_inc(done, 1)

            act.wait_ge(ones_set, 1)
            act.activation(vcol[:, 4, 0:1], ones[:, 0:1], ACT.Sqrt)
            act.wait_ge(w_in[0], 16)
            act.activation(WH[:, 0, 0:UNIT], WR[:, 0, 0:UNIT], ACT.Copy).then_inc(w_hi_done, 1)
            act.wait_ge(tab_in, 16)
            for k in range(KT):
                act.wait_ge(x_in[k], 16)
                act.activation(H[:, 0, k, :], xs[:, k, :], ACT.Copy, scale=cl[:, C_GMIX + k:C_GMIX + k + 1]).then_inc(h_hi, 1)
                if k >= 2:
                    if k >= 4:
                        act.wait_ge(sq_used, k - 3)
                    act.activation(sq[:, k % 2, :], xs[:, k, :], ACT.Square).then_inc(sq_ready, 1)
            root(0, slice(0, 2 * TT), var_ready, std_ready)
            act.wait_ge(dist_set, 3)
            for g in range(3):
                act.dma_start(dist_dram[g], dist_sb[:, g, :].unsqueeze(1).to_broadcast([HEADS, P, DIST])).then_inc(dist_out, 16)
            act.wait_ge(dist_out, 48)
            for t in range(0, TT, 2):
                act.wait_ge(tmA_done, t + 1)
                act.wait_ge(rsb_set, 1)
                act.activation(va0[:, t, :], ps[t][:], ACT.Copy, scale=rs_col[:, t:t + 1]).then_inc(tm_act, 1)
            for g in range(3):
                toeplitz = dist_dram[g].rearrange("h p d -> h (p d)")[:, P - 1:P - 1 + P * (DIST - 1)]
                toeplitz = toeplitz.rearrange("h (p d) -> p h d", d=DIST - 1)[:, :, 0:WIDTH]
                act.dma_start(bias[:, :, g, :], toeplitz).then_inc(bias_in, 16)
            for t in range(0, TT, 2):
                act.wait_ge(tmB_done, t + 1)
                act.activation(v12[:, t, :], ps[t][:], ACT.Copy, scale=rs_col[:, TT + t:TT + t + 1]).then_inc(tm_act, 1)

            def attention(pair):
                jobs = jobs_of(pair)
                base = len(jobs) * pair
                for i in range(len(jobs) + 3):
                    if 0 <= i - 1 < len(jobs):
                        n, (hh, part, t) = base + i - 1, jobs[i - 1]
                        W = P * len(key_tiles(part, t))
                        col = part * 32 + (2 * pair + hh) * TT + t
                        act.wait_ge(m_ready, n + 1)
                        act.activation(T[:, n % 4, 0:W], T[:, n % 4, 0:W], ACT.Exp, scale=-1.0, bias=stats[:, col:col + 1],
                                       accum_out=stats[:, 64 + col:65 + col]).then_inc(p_ready, 1)
                    if 0 <= i - 3 < len(jobs):
                        n, (hh, part, t) = base + i - 3, jobs[i - 3]
                        W = P * len(key_tiles(part, t))
                        act.wait_ge(t_ready, n + 1)
                        if n >= 2:
                            act.wait_ge(pv_done, n - 1)
                        act.activation(pts[:, n % 2, 0:W], ps[6 + n % 2][:, 0:W], ACT.Copy).then_inc(t_free, 1)

            attention(0)

            def gelu2(n, x):
                r = T[:, n % 4, :]
                if len(x.shape) == 3:
                    r = r.rearrange("p (a b) -> p a b", a=x.shape[1])
                act.activation(r, x, ACT.Square).then_inc(g_sq, 1)
                act.wait_ge(g_in, n + 1)
                act.activation(r, r, ACT.Tanh, scale=GELU_B).then_inc(g_th, 1)

            for n in range(4):
                gelu2(n, va0[:, 2 * n:2 * n + 2, 0:WIDTH])
            root(0, slice(0, TT), ln_var, ln_std)
            attention(1)

            def gelu_u(i):
                act.wait_ge(half_free, H_MIX + i + 1)
                gelu2(4 + i, u[:, i // 2, hs_(i % 2)])

            gelu_u(0)
            gelu_u(1)
            act.wait_ge(rowsT_set, 1)
            act.dma_start(stat_dram, rowsT[:]).then_inc(stat_out, 16)
            gelu_u(2)
            gelu_u(3)
            act.wait_ge(stat_out, 16)
            act.dma_start(R[:], stat_dram.rearrange("(s hb t) q -> hb s (t q)", s=4, hb=8)).then_inc(rows_in, 16)
            act.wait_ge(rexp_in, 1)
            for e in (R[:, 0, :], rt[:, 1, :]):
                act.activation(e, e, ACT.Exp).then_inc(rexp_out, 1)
            act.wait_ge(mixw_set, 1)
            for part, e in enumerate((R[:, 0, :], rt[:, 1, :])):
                act.dma_start(mixw_dram[part].rearrange("h (b t) -> (h b) t", b=2), e).then_inc(mixw_out, 16)
            act.wait_ge(mixw_out, 32)
            for part in range(2):
                for head in range(HEADS):
                    rows = slice(64 * (head % 2), 64 * (head % 2) + 64)
                    act.dma_start(wb[rows, part, head // 2, :], mixw_dram[part, head].partition_broadcast(64)).then_inc(wb_in, 16)

            def high(pos, n, ready, val, dst, scale=1.0):
                act.wait_ge(ready, n + 1)
                act.activation(Y[:, 0, 2 * pos + dst[0], dst[1]], val, ACT.Copy, scale=scale).then_inc(y_hi[pos], 1)

            act.wait_ge(pool_ready, 1)
            for q in range(4):
                high(POS_A, q, y_val[POS_A], u[:, q // 2, hs_(q % 2)], (q // 2, hs_(q % 2)), 0.5)
            act.wait_ge(y_val[POS_C], 2)
            for pr in range(BT):
                high(POS_C, pr, y_val[POS_C], O[:, 0, pr, :], (pr, slice(0, S)))
            for q in range(4):
                high(POS_D, q, dmm_done, ps[4 + q][:], (q // 2, hs_(q % 2)), cl[:, C_DSC + q // 2:C_DSC + q // 2 + 1])
            for q in range(4):
                high(POS_B, q, y_val[POS_B], cv[:, q // 2, hs_(q % 2)], (q // 2, hs_(q % 2)))

            def gate_tanh(n):
                act.wait_ge(half_free, H_GATE + n + 1)
                act.activation(T[:, n % 4, :], T[:, n % 4, :], ACT.Tanh, scale=0.5).then_inc(tanh_done, 1)

            for n in range(2 * N_GATE - 1):
                gate_tanh(n)

            def reload_x(n):
                if n >= 2:
                    act.wait_ge(half_free, H_WO + n - 1)
                act.dma_start(T[:, 2 + n % 2, :], xT[(n // 2) * P:(n // 2 + 1) * P, hs_(n % 2)]).then_inc(xr_in[n % 2], 16)

            act.wait_ge(half_done, H_WO)
            act.wait_ge(m_set, 2 * KT - 2)
            for n in range(2 * KT):
                h, k = divmod(n, KT)
                if n == 2:
                    gate_tanh(2 * N_GATE - 1)
                if n == KT - 1:
                    act.wait_ge(m_set, 2 * KT - 1)
                if n == KT:
                    act.wait_ge(m_set, 2 * KT)
                    reload_x(0)
                    reload_x(1)
                act.activation(H[:, 0, k, hs_(h)], M[:, k, hs_(h)], ACT.Copy).then_inc(m_hi, 1)
            for n in range(2 * KT):
                j, h = n // 2, n % 2
                act.wait_ge(half_free, H_WO + n + 1)
                act.activation(Y[:, 0, j, hs_(h)], M[:, j, hs_(h)], ACT.Copy, scale=cl[:, C_GFF + j:C_GFF + j + 1]).then_inc(xg_hi, 1)
                if n >= 2:
                    act.wait_ge(x2_sum, n - 1)
                act.activation(T[:, n % 2, :], M[:, j, hs_(h)], ACT.Square).then_inc(x2_sq, 1)
                if n + 2 < 2 * KT:
                    reload_x(n + 2)
            root(1, slice(0, 2 * TT), var_ready, std_ready)

            for c in range(CHUNKS):
                for n in range(2 * KT):
                    act.wait_ge(half_free, H_FF + 4 * KT * c + n + 1)
                    r = T[:, n % 4, :]
                    link(act.activation(r, r, ACT.Square))
                    act.activation(H[:, 0, n // 2, hs_(n % 2)], r, ACT.Copy).then_inc(f_hi, 1)

            def final_factor(h):
                root(2 + h, slice(4 * h, 4 * h + 4), var_ready, std_ready)
                act.wait_ge(rsb_ps, 5 + h)
                act.activation(rs_b[:, hs_(h)], ps[6 + h][:], ACT.Copy).then_inc(rsb_set, 1)

            for n in range(2 * KT):
                m = M[:, n // 2, hs_(n % 2)]
                act.wait_ge(half_free, H_FF + 4 * KT * (CHUNKS - 1) + 2 * KT + n + 1)
                if n >= 2:
                    act.wait_ge(x3_sum, n - 1)
                act.activation(T[:, n % 2, :], m, ACT.Square).then_inc(x3_sq, 1)
                act.activation(m, m, ACT.Copy, scale=cl[:, C_GFIN + n // 2:C_GFIN + n // 2 + 1]).then_inc(x3_g, 1)
                if n == 2 * KT - 2:
                    final_factor(0)
            final_factor(1)
            for i, m in enumerate(OUT_POOL[1]):
                act.wait_ge(out_pool, len(OUT_POOL[0]) + i + 1)
                act.dma_start(out[m * P:(m + 1) * P, hs_(1)], M[:, m, hs_(1)]).then_inc(out_sent, 16)


def key_tiles(part, t):
    if part == 0:
        return [(0, k) for k in range(max(t - 1, 0), t + 1)]
    blk, r = divmod(t, 4)
    return [(g, 4 * b + r) for g in range(2) for b in range(blk + 1)]


def t5_bucket(dist):
    exact = BUCKETS // 2
    d = np.maximum(dist, 1).astype(np.float32)
    large = exact + (np.log(d / np.float32(exact)) / np.float32(np.log(2048 / exact)) * (BUCKETS - exact)).astype(np.int32)
    return np.where(dist < exact, dist, np.minimum(large, BUCKETS - 1))


def distance_onehot():
    e = np.zeros((BUCKETS + 1, 3, DIST), np.float32)
    for g, dil in enumerate((1, 4, 16)):
        for i in range(DIST):
            diff = 255 - i
            step = 4 if g == 2 else 1
            ok = 0 <= diff <= P * step and diff % step == 0
            row = int(t5_bucket(np.array(diff // step * dil))) if ok else BUCKETS
            e[row, g, i] = 1.0
    return e


def kernel(**inputs):
    import concourse.bacc as bacc
    from concourse.bass_utils import run_bass_kernel_spmd as run

    a = {k: np.asarray(v) for k, v in inputs.items()}
    w_in = a["w_in"][0]
    cuts = np.cumsum([0, WIDTH, WIDTH, WIDTH, WIDTH, WIDTH, 768, 768, 768, WIDTH])
    A_U, A_V, B_B, B_C, B_X, C_Q, C_K, C_V, D_Z, GATES = (int(x) for x in cuts)

    def block(w, c):
        return w[:, c:c + P].reshape(-1, P, P).transpose(1, 0, 2).reshape(P, -1)

    units = []
    for pair in range(2):
        qk = [block(w_in, base + g * WIDTH + pair * P) for g in range(3) for base in (C_Q, C_K)]
        units += qk
        if pair == 0:
            for wide in (np.concatenate([w_in[:, A_V:A_V + WIDTH], w_in[:, C_V:C_V + WIDTH]], 1),
                         w_in[:, C_V + WIDTH:C_V + 3 * WIDTH]):
                units += [w.transpose(1, 0, 2).reshape(P, UNIT) for w in wide.reshape(4, 2, P, HALF)]
    units += [block(w_in, base + m * P) for base in (A_U, D_Z, B_C, B_X, B_B) for m in range(BT)]
    w1 = np.stack(units)
    outs = {POS_A: a["w_a_out"][0], POS_B: a["w_b_out"][0], POS_C: a["w_c_out"][0], POS_D: a["w_d_out"][0]}
    w2 = np.stack([np.concatenate([block(w_in, GATES + REF_GATE[pos] * D + j * P), block(outs[pos], j * P)], 1)
                   for j in range(KT) for pos in GATE_ORDER])
    f1, f2 = a["w_ff1"][0], a["w_ff2"][0]
    units = [block(a["w_o"][0], j * P) for j in range(KT)]
    for c in range(CHUNKS):
        units += [block(f1, c * D + m * P) for m in range(KT)]
        units += [block(f2[c * D:(c + 1) * D], m * P) for m in range(KT)]
    w3 = np.stack(units)

    cols = np.zeros((P, N_COLS), np.float32)
    cols[:, C_GMIX:C_GMIX + KT] = a["norm_mix_g"][0].reshape(KT, P).T
    cols[:, C_GFF:C_GFF + KT] = a["norm_ff_g"][0].reshape(KT, P).T
    cols[:, C_GFIN:C_GFIN + KT] = a["final_g"].reshape(KT, P).T
    cols[:, C_CONV:C_CONV + 6] = a["b_conv"][0].reshape(3 * BT, P).T
    cols[:, C_DSC:C_DSC + BT] = a["d_scale"][0].reshape(BT, P).T
    windows = np.repeat(np.array([2, 4, 8, 16], np.float32), 64).reshape(BT, P)
    cols[:, C_WINV:C_WINV + BT] = (1 / windows).T
    t = np.arange(1, 17, dtype=np.float32)
    cols[:, C_RATIO:] = (windows[:, :, None] / np.minimum(t, windows[:, :, None])).transpose(1, 0, 2).reshape(P, -1)

    arrays = {
        "xT": np.ascontiguousarray(a["x"][0].T), "cols": cols, "eye": np.eye(P, dtype=np.float32),
        "onehot": distance_onehot(), "rel": a["rel_bias"],
        "lnrow": np.stack([a["a_ln_g"][0], a["a_ln_b"][0]]), "bsrow": a["a_bs"][0],
        "wsT": np.ascontiguousarray(a["a_ws"][0].transpose(2, 0, 1)), "dw": a["d_w"][0],
        "w1": w1, "w2": w2, "w3": w3,
    }
    nc = bacc.Bacc("TRN2", target_bir_lowering=False, num_devices=1)
    aps = [nc.dram_tensor(f"in_{n}", v.shape, mybir.dt.from_np(v.dtype), kind="ExternalInput").ap() for n, v in arrays.items()]
    outT = nc.dram_tensor("outT", (D, S), F32, kind="ExternalOutput").ap()
    build(nc, *aps, outT)
    r = run(nc, [{f"in_{n}": v for n, v in arrays.items()}], core_ids=[0])
    return r.results[0]["outT"].T.reshape(1, S, D)
```

```python
from contextlib import ExitStack

import numpy as np

import concourse.bass as bass
from concourse import mybir

ALU = mybir.AluOpType
ACT = mybir.ActivationFunctionType
AX = mybir.AxisListType
F32 = mybir.dt.float32
F32R = mybir.dt.float32r

P = 128
D = 1024
S = 1024
KT = D // P
TT = S // P
HALF = 512
NH = S // HALF
WIDTH = 256
BT = WIDTH // P
HEADS = 4
DH = 64
FF = 4 * D
CHUNKS = FF // D
EPS = 1e-6
NEG = -1e30
BUCKETS = 32
DIST = 384
GELU_A, GELU_B = 0.044715, 0.7978845608028654
UNIT = KT * P
GUNIT = UNIT + BT * P
KB = 256

C_GMIX, C_GFF, C_GFIN = 0, 8, 16
C_CONV, C_DSC, C_WINV = 24, 30, 32
C_RATIO = 34
N_COLS = 66

N_QK, N_TM = 6, 8
U_TM = N_QK
U_QK1 = U_TM + N_TM
U_MIX = U_QK1 + N_QK
N_MIX = 10
U_GATE = U_MIX + N_MIX
N_GATE = 4 * KT
U_WO = U_GATE + N_GATE
U_FF = U_WO + KT
N_UNITS = U_FF + 2 * KT * CHUNKS
H_QK1 = 2 * N_QK
H_MIX = 2 * H_QK1
H_GATE = H_MIX + 2 * N_MIX
H_WO = H_GATE + 2 * N_GATE
H_FF = H_WO + 2 * KT
OUT_POOL = ((0, 1, 2, 3, 4), (0, 1, 2))
OUT_DVE = tuple(tuple(m for m in range(KT) if m not in tiles) for tiles in OUT_POOL)
OUT_SENT = [(0, m) for m in (0, 5, 1, 6, 2, 3, 7, 4)] + [(1, m) for m in OUT_DVE[1]]
POOL_LOWS = (2, 4, 6)
DVE_LOWS = [(h, k) for h in range(NH) for k in range(KT) if h or k not in POOL_LOWS]
POS_B, POS_A, POS_D, POS_C = 0, 1, 2, 3
GATE_ORDER = (POS_A, POS_B, POS_D, POS_C)
REF_GATE = {POS_A: 0, POS_B: 1, POS_C: 2, POS_D: 3}


AHEAD = 4


def jobs_of(pair):
    start = [(0, part, t) for part in range(2) for t in range(AHEAD)]
    return start + [(hh, part, t) for hh in range(2) for t in range(0 if hh else AHEAD, TT) for part in range(2)]


def build(nc, xT, cols, eye, onehot, rel, lnrow, bsrow, wsT, dw, w1, w2, w3, out):
    ctx = ExitStack()
    with ctx:
        def sb(name, shape, dt=F32):
            return ctx.enter_context(nc.sbuf_tensor(name, shape, dt))

        def sem(name):
            return ctx.enter_context(nc.semaphore(name))

        H = sb("act_split", [P, 2, KT, S], F32R)
        WR = sb("w_raw", [P, 2, GUNIT])
        WH = sb("w_hi", [P, 2, GUNIT], F32R)
        WL = sb("w_lo", [P, 2, GUNIT], F32R)
        rs_b = sb("rs_b", [P, S])
        with ExitStack() as inner:
            diag = inner.enter_context(nc.sbuf_tensor("diagonals", [P, 4, HALF], F32R))
        T = sb("ring", [P, 4, HALF])
        sqacc = sb("sqacc", [P, S])
        cl = sb("cols_sb", [P, N_COLS])
        ident = sb("ident", [P, P])
        ones = sb("ones", [P, 1])
        ones_r = sb("ones_r", [P, P], F32R)
        vcol = sb("vcol", [P, 5, TT])
        rs_hi = sb("rs_hi", [P, TT], F32R)
        rs_lo = sb("rs_lo", [P, TT], F32R)
        rs_col = sb("rs_col", [P, 2 * TT])

        def place(name, kib, shape, dt=F32):
            with ExitStack() as inner:
                if kib:
                    inner.enter_context(nc.sbuf_tensor(f"below_{name}", [P, int(kib * KB)], F32))
                return inner.enter_context(nc.sbuf_tensor(name, shape, dt))

        Y = place("branch_split", 0, [P, 2, KT, S], F32R)
        M = place("merged", 64, [P, KT, S])
        xs = place("xs", 0, [P, KT, S])
        sq = place("sq", 32, [P, 2, S])
        sqp = place("sq_pool", 40, [P, 2, S])
        onehot_sb = place("onehot_sb", 80, [BUCKETS + 1, 3, DIST])
        rel_sb = place("rel_sb", 90, [BUCKETS + 1, 12])
        dist_sb = place("dist_sb", 85, [HEADS, 3, DIST])
        qk = place("qk", 0, [P, 6, S])
        v12 = place("v12", 24, [P, TT, HALF])
        bias = place("bias", 40, [P, HEADS, 3, WIDTH])
        pts = place("pts", 52, [P, 2, HALF])
        stats = place("stats", 56, [P, P])
        rowsT = place("rowsT", 56.5, [P, P])
        small = place("ln_stats", 57, [P, TT, 8])
        ws_sb = place("ws_sb", 58, [P, 4, P])
        dw_sb = place("dw_sb", 60, [P, BT, P])
        ln_sb = place("ln_sb", 61, [P, 2, WIDTH])
        bs_sb = place("bs_sb", 63, [P, BT, P])
        O = place("attn_out", 64, [P, 2, 2, S])
        va0 = place("va0", 80, [P, TT, HALF])
        R = place("rows", 0, [8, 4, HALF])
        rt = place("row_tmp", 8, [8, 2, HALF])
        sA = place("pool_a", 12, [P, S])
        wb = place("mix_w", 16, [P, 2, 2, S])
        u = place("gmlp_u", 40, [P, BT, S])
        tc = place("conv_in", 32, [P, BT, S])
        cv = place("conv_out", 72, [P, BT, S])
        z = place("pool_z", 48, [P, BT, S])

        ps = [ctx.enter_context(nc.psum_tensor(f"bank{i}", [P, HALF], F32)) for i in range(8)]

        dist_dram = nc.dram_tensor("dist_scratch", [3, HEADS, P, DIST], F32, kind="Internal").ap()
        stat_dram = nc.dram_tensor("stat_scratch", [P, P], F32, kind="Internal").ap()
        mixw_dram = nc.dram_tensor("mixw_scratch", [2, HEADS, S], F32, kind="Internal").ap()

        x_in = [sem(f"x_in{k}") for k in range(KT)]
        w_in = [sem(f"w_in{i}") for i in range(2)]
        tab_in, onehot_in, rel_in = sem("tab_in"), sem("onehot_in"), sem("rel_in")
        ones_set, rel_set, dw_zero, ws_masked = sem("ones_set"), sem("rel_set"), sem("dw_zero"), sem("ws_masked")
        w_hi_done, w_split, w_used = sem("w_hi_done"), sem("w_split"), sem("w_used")
        h_hi, h_lo, sq_ready, sq_used = sem("h_hi"), sem("h_lo"), sem("sq_ready"), sem("sq_used")
        ssq_ps, var_ready, std_ready = sem("ssq_ps"), sem("var_ready"), sem("std_ready")
        diag_ready, rsb_ps, rsb_set = sem("diag_ready"), sem("rsb_ps"), sem("rsb_set")
        dist_ps, dist_set, dist_out, bias_in = sem("dist_ps"), sem("dist_set"), sem("dist_out"), sem("bias_in")
        half_done, half_free = sem("half_done"), sem("half_free")
        tmA_done, tmB_done = sem("tmA_done"), sem("tmB_done")
        tm_dve, tm_act = sem("tm_dve"), sem("tm_act")
        s_ready, m_ready, p_ready = sem("s_ready"), sem("m_ready"), sem("p_ready")
        t_ready, t_free, pv_done, o_free = sem("t_ready"), sem("t_free"), sem("pv_done"), sem("o_free")
        statsT_ps, rowsT_set, rows_in = sem("statsT_ps"), sem("rowsT_set"), sem("rows_in")
        rexp_in, rexp_out, mixw_set, mixw_out = (sem(n) for n in ("rexp_in", "rexp_out", "mixw_set", "mixw_out"))
        g_sq, g_in, g_th = sem("g_sq"), sem("g_in"), sem("g_th")
        ln_var, ln_std, v_ready = sem("ln_var"), sem("ln_std"), sem("v_ready")
        sv_done, sv_free = sem("sv_done"), sem("sv_free")
        pool_ready, dmm_done = sem("pool_ready"), sem("dmm_done")
        y_val = [sem(f"y_val{i}") for i in range(4)]
        y_hi = [sem(f"y_hi{i}") for i in range(4)]
        y_lo = [sem(f"y_lo{i}") for i in range(4)]
        tanh_done, y_ps, y_free, m_set = sem("tanh_done"), sem("y_ps"), sem("y_free"), sem("m_set")
        m_hi, m_lo, m_lo_pool = sem("m_hi"), sem("m_lo"), sem("m_lo_pool")
        xr_in = [sem(f"xr_in{i}") for i in range(2)]
        xg_hi, xg_lo, x2_sq, x2_sum = sem("xg_hi"), sem("xg_lo"), sem("x2_sq"), sem("x2_sum")
        f_sq, f_hi, f_lo = sem("f_sq"), sem("f_hi"), sem("f_lo")
        x3_sq, x3_g, out_dve, out_pool, out_sent = sem("x3_sq"), sem("x3_g"), sem("out_dve"), sem("out_pool"), sem("out_sent")
        dve_chain, rs_strided = sem("dve_chain"), sem("rs_strided")
        x3_sum, ident_in, ws_in, mix_in = (sem(n) for n in ("x3_sum", "ident_in", "ws_in", "mix_in"))
        stat_out, wb_in = sem("stat_out"), sem("wb_in")
        pool_sq, pool_sq_part = sem("pool_sq"), sem("pool_sq_part")

        w_head_in, w_head_hi, w_head_split = sem("w_head_in"), sem("w_head_hi"), sem("w_head_split")

        MIX_DMAS = 9
        HEAD_COLS = 2 * P
        w_head, w_body = slice(0, HEAD_COLS), slice(HEAD_COLS, UNIT)
        S_BANKS = (2, 3, 4, 5)

        def bank_of(hs):
            return ps[hs % 6 if hs < H_QK1 else (hs + 2) % 4][:]

        def zz(q):
            return z[:, q // 2, hs_(q % 2)]

        block = ctx.enter_context(nc.Block())

        def hs_(h):
            return slice(h * HALF, (h + 1) * HALF)

        def strided(t):
            blk, r = divmod(t, 4)
            return slice(blk * HALF + r, (blk + 1) * HALF, 4)

        @block.sync
        def _(sp):
            def weights(src, i, slot, n):
                sp.dma_start(WR[:, slot, 0:n], src[i]).then_inc(w_in[slot], 16)

            def stream(src, skip, u0, count, n):
                with sp.Fori(skip // 2, count // 2) as i:
                    for slot in range(2):
                        sp.wait_ge(w_split, 2 * i + (u0 + slot - 1))
                        weights(src, 2 * i + slot, slot, n)

            sp.dma_start(cl[:], cols).then_inc(tab_in, 16)
            sp.dma_start(WR[:, 0, 0:HEAD_COLS], w1[0, :, 0:HEAD_COLS]).then_inc(w_head_in, 16)
            for k in range(KT):
                sp.dma_start(xs[:, k, :], xT[k * P:(k + 1) * P, :]).then_inc(x_in[k], 16)
                if k == 0:
                    sp.dma_start(WR[:, 0, HEAD_COLS:UNIT], w1[0, :, HEAD_COLS:UNIT]).then_inc(w_in[0], 16)
                if k == 2:
                    weights(w1, 1, 1, UNIT)
            sp.dma_start(ident[:], eye).then_inc(ident_in, 16)
            sp.dma_start(onehot_sb[:], onehot).then_inc(onehot_in, 16)
            sp.dma_start(rel_sb[0:BUCKETS, :], rel).then_inc(rel_in, 16)
            sp.dma_start(ws_sb[:], wsT).then_inc(ws_in, 16)
            sp.dma_start(ln_sb[:], lnrow.partition_broadcast(P)).then_inc(mix_in, 16)
            sp.wait_ge(dw_zero, 1)
            for g in range(4):
                rows = slice(64 * (g % 2), 64 * (g % 2) + 64)
                sp.dma_start(dw_sb[rows, g // 2, rows], dw[g]).then_inc(mix_in, 16)
                sp.dma_start(bs_sb[rows, g // 2, :], bsrow[g].partition_broadcast(64)).then_inc(mix_in, 16)

            stream(w1, 2, 0, U_GATE, UNIT)
            stream(w2, 0, U_GATE, N_GATE, GUNIT)
            stream(w3, 0, U_WO, N_UNITS - U_WO, UNIT)
            done = {OUT_DVE: 0, OUT_POOL: 0}
            for h, m in OUT_SENT:
                by, scaled = (OUT_DVE, out_dve) if m in OUT_DVE[h] else (OUT_POOL, out_pool)
                done[by] += 1
                sp.wait_ge(scaled, done[by])
                sp.dma_start(out[m * P:(m + 1) * P, hs_(h)], M[:, m, hs_(h)]).then_inc(out_sent, 16)
            sp.wait_ge(out_sent, 16 * KT * NH)

        @block.gpsimd
        def _(pool):
            def unit_used(u):
                if u < U_TM:
                    pool.wait_ge(half_done, 2 * u + 2)
                elif u < U_QK1:
                    part, i = divmod(u - U_TM, 4)
                    if i < 3:
                        pool.wait_ge(w_used, 3 * part + i + 1)
                    else:
                        pool.wait_ge(tmB_done if part else tmA_done, TT)
                else:
                    pool.wait_ge(half_done, H_QK1 + 2 * (u - U_QK1) + 2)

            def split(u, n, more=0):
                slot = u % 2
                pool.wait_ge(w_in[slot], 8 * more + 16 * (u // 2 + 1))
                raw, hi, lo = WR[:, slot, 0:n], WH[:, slot, 0:n], WL[:, slot, 0:n]
                pool.tensor_tensor(hi, raw, ones[:, 0:1].to_broadcast([P, n]), ALU.mult).then_inc(w_hi_done, 1)
                pool.wait_ge(w_hi_done, more + (u + 1))
                pool.tensor_tensor(lo, raw, hi.bitcast(F32), ALU.subtract).then_inc(w_split, 1)

            pool.wait_ge(ones_set, 1)
            def square_x(k):
                pool.wait_ge(x_in[k], 16)
                pool.tensor_tensor(sqp[:, k, :], xs[:, k, :], xs[:, k, :], ALU.mult).then_inc(pool_sq_part, 1)

            square_x(0)
            pool.wait_ge(w_split, 1)
            split(1, UNIT)
            square_x(1)
            pool.wait_ge(pool_sq_part, 2)
            pool.tensor_tensor(sqp[:, 0, :], sqp[:, 0, :], sqp[:, 1, :], ALU.add).then_inc(pool_sq, 1)
            pool.wait_ge(ws_in, 16)
            pool.affine_select(out=ws_sb[:], in_=ws_sb[:], compare_op=ALU.is_ge, fill=0.0, base=0,
                               pattern=[[0, 4], [1, P]], channel_multiplier=-1).then_inc(ws_masked, 1)
            for u_ in range(2, U_GATE + 2):
                unit_used(u_ - 2)
                split(u_, GUNIT if u_ >= U_GATE else UNIT)
            with pool.Fori(1, N_GATE // 2) as i:
                for slot in range(2):
                    pool.wait_ge(y_ps, 4 * i + (2 * slot - 2))
                    split(U_GATE + slot, GUNIT, 2 * i)
            pool.wait_ge(y_ps, 2 * N_GATE - 2)
            split(U_WO, UNIT)
            for k in POOL_LOWS:
                pool.wait_ge(m_hi, k + 1)
                h0 = hs_(0)
                pool.tensor_tensor(H[:, 1, k, h0], M[:, k, h0], H[:, 0, k, h0].bitcast(F32), ALU.subtract).then_inc(m_lo_pool, 1)
            pool.wait_ge(y_ps, 2 * N_GATE)
            split(U_WO + 1, UNIT)
            with pool.Fori(1, (N_UNITS - U_WO) // 2) as i:
                for slot in range(2):
                    pool.wait_ge(half_done, 4 * i + (H_WO + 2 * slot - 2))
                    split(U_WO + slot, UNIT, 2 * i)
            for h in range(NH):
                pool.wait_ge(rsb_set, 3 + h)
                for m in OUT_POOL[h]:
                    pool.wait_ge(x3_g, 2 * m + h + 1)
                    pool.tensor_tensor(M[:, m, hs_(h)], M[:, m, hs_(h)], rs_b[:, hs_(h)], ALU.mult).then_inc(out_pool, 1)

        @block.tensor
        def _(pe):
            def split_mm(bank, w, slot, wcol, acts, ak, sl, first, last):
                wh, wl = WH[:, slot, wcol:wcol + P], WL[:, slot, wcol:wcol + P]
                pe.matmul(bank, wh, acts[:, 0, ak, sl], start=first, stop=False)
                pe.matmul(bank, wh, acts[:, 1, ak, sl], start=False, stop=False)
                return pe.matmul(bank, wl, acts[:, 0, ak, sl], start=False, stop=last)

            def unit(u, hs, acts, before=None, at={}, more=0):
                pe.wait_ge(w_split, more + (u + 1))
                for h in range(NH):
                    if hs >= H_QK1:
                        pe.wait_ge(half_free, 2 * more + (hs + h - 3))
                    elif hs >= 6:
                        pe.wait_ge(half_free, hs + h - 5)
                    for k in range(KT):
                        if before:
                            before(k, h)
                        if (k, h) in at:
                            at[k, h]()
                        mm = split_mm(bank_of(hs + h), WH, u % 2, k * P, acts, k, hs_(h), k == 0, k == KT - 1)
                    mm.then_inc(half_done, 1)

            def column_sums(ready, n):
                pe.wait_ge(ready, n)
                for c in range(TT):
                    mm = pe.matmul(ps[6][:, c:c + 1], sqacc[:, c * P:(c + 1) * P], ones[:, 0:1], start=True, stop=True)
                mm.then_inc(ssq_ps, 1)

            def spread(h, n, slot):
                pe.wait_ge(diag_ready, n)
                for part in range(2):
                    mm = pe.matmul(ps[6 + h][:], ones_r[:], diag[:, slot + part, :], start=not part, stop=bool(part))
                mm.then_inc(rsb_ps, 1)


            pe.wait_ge(w_head_split, 1)
            for u_, k in ((0, 0), (0, 1), (0, 2), (0, 3), (1, 0), (1, 1), (0, 4), (1, 2), (0, 5), (1, 3), (0, 6), (0, 7),
                          (1, 4), (1, 5), (1, 6), (1, 7)):
                if u_ == 0:
                    if k * P == HEAD_COLS:
                        pe.wait_ge(w_split, 1)
                    pe.wait_ge(h_hi, k + 1)
                    for h in range(NH):
                        for w in (WH, WL):
                            pe.matmul(bank_of(h), w[:, 0, k * P:(k + 1) * P], H[:, 0, k, hs_(h)], start=k == 0 and w is WH, stop=False)
                    pe.wait_ge(h_lo, k + 1)
                    for h in range(NH):
                        mm = pe.matmul(bank_of(h), WH[:, 0, k * P:(k + 1) * P], H[:, 1, k, hs_(h)], start=False, stop=k == KT - 1)
                        if k == KT - 1:
                            mm.then_inc(half_done, 1)
                    continue
                if k == 0:
                    pe.wait_ge(w_split, 2)
                for h in range(NH):
                    mm = split_mm(bank_of(2 + h), WH, 1, k * P, H, k, hs_(h), k == 0, k == KT - 1)
                    if k == KT - 1:
                        mm.then_inc(half_done, 1)
            pe.wait_ge(ones_set, 2)
            unit(2, 4, H, at={
                (0, 0): lambda: column_sums(sq_used, KT - 1),
                (1, 1): lambda: spread(0, 1, 0), (3, 1): lambda: spread(1, 2, 2)})
            pe.wait_ge(rsb_set, 1)
            pe.wait_ge(onehot_in, 16)
            pe.wait_ge(rel_set, 1)
            pe.wait_ge(rel_in, 16)

            def distances(g):
                pe.matmul(ps[6 + g % 2][0:HEADS, 0:DIST], rel_sb[:, g * HEADS:(g + 1) * HEADS],
                          onehot_sb[:, g, :], start=True, stop=True).then_inc(dist_ps, 1)

            distances(0)
            distances(1)
            unit(3, 6, H)
            pe.wait_ge(dist_set, 1)
            distances(2)
            unit(4, 8, H)
            unit(5, 10, H)

            def attention(pair):
                jobs = jobs_of(pair)
                base = len(jobs) * pair

                def scores(i):
                    n, (hh, part, t) = base + i, jobs[i]
                    if n >= 4:
                        pe.wait_ge(m_ready, n - 3)
                    rows = slice(64 * hh, 64 * hh + DH)
                    bank = ps[S_BANKS[n % 4]]
                    if part == 0:
                        ks = slice(max(t - 1, 0) * P, (t + 1) * P)
                        W = P if t == 0 else 2 * P
                        mm = pe.matmul(bank[:, 0:W], qk[rows, 0, t * P:(t + 1) * P], qk[rows, 1, ks], start=True, stop=True)
                    else:
                        blk, r = divmod(t, 4)
                        W = P * (blk + 1)
                        for g in range(2):
                            mm = pe.matmul(bank[:, g * W:(g + 1) * W], qk[rows, 2 + 2 * g, strided(t)],
                                           qk[rows, 3 + 2 * g, r:(blk + 1) * HALF:4], start=True, stop=True)
                    mm.then_inc(s_ready, 1)

                def turn(i):
                    n, (hh, part, t) = base + i, jobs[i]
                    pe.wait_ge(p_ready, n + 1)
                    if n >= 2:
                        pe.wait_ge(t_free, n - 1)
                    for c in range(len(key_tiles(part, t))):
                        mm = pe.transpose(ps[6 + n % 2][:, c * P:(c + 1) * P], T[:, n % 4, c * P:(c + 1) * P], ident[:])
                    mm.then_inc(t_ready, 1)

                def weighted(i):
                    n, (hh, part, t) = base + i, jobs[i]
                    pe.wait_ge(t_free, n + 1)
                    if n >= 2:
                        pe.wait_ge(o_free, n - 1)
                    head = 2 * pair + hh
                    kts = key_tiles(part, t)
                    for c, (g, kt) in enumerate(kts):
                        v = va0[:, kt, WIDTH + head * DH:WIDTH + (head + 1) * DH] if part == 0 else \
                            v12[:, kt, g * WIDTH + head * DH:g * WIDTH + (head + 1) * DH]
                        mm = pe.matmul(ps[n % 2][64 * hh:64 * hh + DH, 0:P], v, pts[:, n % 2, c * P:(c + 1) * P],
                                       start=(c == 0), stop=(c == len(kts) - 1))
                    mm.then_inc(pv_done, 1)

                def step(i):
                    if i < len(jobs):
                        scores(i)
                    if 0 <= i - 3 < len(jobs):
                        turn(i - 3)
                    if 0 <= i - 4 < len(jobs):
                        weighted(i - 4)

                def main(rest_of_keys=None):
                    turn(0)
                    if rest_of_keys:
                        rest_of_keys()
                    scores(4)
                    turn(1)
                    weighted(0)
                    for i in range(AHEAD + 1, len(jobs)):
                        step(i)

                return scores, main, {(k, 0): lambda i=i: step(len(jobs) + i) for i, k in enumerate((1, 3, 5, 7))}

            scores, main, rest = attention(0)
            for part in range(2):
                for i in range(4):
                    u_ = U_TM + 4 * part + i
                    pe.wait_ge(w_split, u_ + 1)
                    for t in range(TT):
                        if i == 0 and part == 0:
                            if t < 6:
                                pe.wait_ge(half_free, 7 + t)
                            else:
                                pe.wait_ge(dist_set, 2 if t == 7 else 3)
                        if i == 0 and part == 1:
                            pe.wait_ge(tm_dve if t % 2 else tm_act, t // 2 + 1)
                        toks = slice(t * P, (t + 1) * P) if part == 0 else strided(t)
                        for kk in range(2):
                            k = 2 * i + kk
                            hi, lo = H[:, 0, k, toks], H[:, 1, k, toks]
                            wh, wl = (w[:, u_ % 2, kk * HALF:(kk + 1) * HALF] for w in (WH, WL))
                            pe.matmul(ps[t][:], hi, wh, start=(k == 0), stop=False)
                            pe.matmul(ps[t][:], hi, wl, start=False, stop=False)
                            mm = pe.matmul(ps[t][:], lo, wh, start=False, stop=(k == KT - 1))
                        if i == 3:
                            mm.then_inc(tmB_done if part else tmA_done, 1)
                            if part and t >= TT - AHEAD:
                                i_ = t - (TT - AHEAD)
                                pe.wait_ge(tm_dve if i_ % 2 else tm_act, TT // 2 + 2 + i_ // 2)
                                if i_ == 0:
                                    pe.wait_ge(half_free, 2 * N_QK)
                                scores(i_)
                    if i < 3:
                        mm.then_inc(w_used, 1)

            pe.wait_ge(tm_dve, TT)
            pe.wait_ge(tm_act, TT)
            main()
            pe.wait_ge(m_ready, 30)
            unit(U_QK1, H_QK1, H, at=rest)
            pe.wait_ge(o_free, 32)
            for i in range(1, N_QK - 1):
                unit(U_QK1 + i, H_QK1 + 2 * i, H)
            scores, main, rest = attention(1)

            def scores_ahead(i):
                if i == 0:
                    pe.wait_ge(half_free, H_MIX - 2)
                scores(i)

            unit(U_QK1 + N_QK - 1, H_MIX - 2, H, at={(2 * i, 1): lambda i=i: scores_ahead(i) for i in range(AHEAD)})
            main(lambda: pe.wait_ge(half_free, H_MIX))
            pe.wait_ge(m_ready, 62)
            unit(U_MIX, H_MIX, H, at=rest)
            pe.wait_ge(o_free, 64)
            pe.wait_ge(t_free, 64)
            pe.transpose(ps[7][:, 0:P], stats[:], ident[:]).then_inc(statsT_ps, 1)
            unit(U_MIX + 1, H_MIX + 2, H)
            unit(U_MIX + 2, H_MIX + 4, H)
            pe.wait_ge(v_ready, 1)
            pe.wait_ge(mix_in, 16 * MIX_DMAS)
            pe.wait_ge(ws_masked, 1)
            pe.wait_ge(rowsT_set, 1)
            for pr in range(BT):
                for h in range(NH):
                    for c in range(4):
                        for gg in range(2):
                            g = 2 * pr + gg
                            mm = pe.matmul(ps[4 + 2 * pr + h][64 * gg:64 * gg + 64, c * P:(c + 1) * P],
                                           va0[:, 4 * h + c, g * 64:(g + 1) * 64], ws_sb[:, g, :], start=True, stop=True)
                    mm.then_inc(sv_done, 1)
            for i in range(3, 8):
                unit(U_MIX + i, H_MIX + 2 * i, H)
            pe.wait_ge(pool_ready, 1)
            pe.wait_ge(sv_free, 4)
            for tile in range(BT):
                for h in range(NH):
                    pe.matmul(ps[4 + 2 * tile + h][:], dw_sb[:, tile, :], z[:, tile, hs_(h)],
                              start=True, stop=True).then_inc(dmm_done, 1)
            for i in range(8, N_MIX):
                unit(U_MIX + i, H_MIX + 2 * i, H)

            def gates(j, first):
                for b, pos in enumerate(GATE_ORDER):
                    slot = b % 2
                    pe.wait_ge(w_split, 4 * j + (U_GATE + b + 1))
                    for h in range(NH):
                        n = 2 * b + h
                        pe.wait_ge(half_free, 8 * j + (H_GATE + n - 3))
                        for k in range(KT):
                            mm = split_mm(bank_of(H_GATE + n), WH, slot, k * P, H, k, hs_(h), k == 0, k == KT - 1)
                        mm.then_inc(half_done, 1)
                        if first:
                            if n == 0:
                                pe.wait_ge(y_lo[POS_D], 4)
                            pe.wait_ge(y_lo[pos], 2 if pos == POS_C else 4)
                        if n >= 2 or not first:
                            pe.wait_ge(y_free, 8 * j + (n - 1))
                        for k in range(BT):
                            mm = split_mm(ps[4 + n % 2][:], WH, slot, UNIT + k * P, Y, 2 * pos + k, hs_(h), k == 0, k == BT - 1)
                        mm.then_inc(y_ps, 1)

            gates(0, True)
            with pe.Fori(1, KT) as j:
                gates(j, False)

            def merged_split(k, h):
                if (h, k) in DVE_LOWS:
                    pe.wait_ge(m_lo, DVE_LOWS.index((h, k)) + 1)
                else:
                    pe.wait_ge(m_lo_pool, POOL_LOWS.index(k) + 1)

            unit(U_WO, H_WO, H, merged_split)
            unit(U_WO + 1, H_WO + 2, H)
            with pe.Fori(1, KT // 2) as i:
                unit(U_WO, H_WO, H, more=2 * i)
                unit(U_WO + 1, H_WO + 2, H, more=2 * i)

            def most_squares(h):
                pe.wait_ge(x3_sum, 2 * KT - 3 + h)
                for c in range(TT // NH):
                    pe.matmul(ps[6 + h][:, c:c + 1], sqacc[:, h * HALF + c * P:h * HALF + (c + 1) * P], ones[:, 0:1],
                              start=c == 0, stop=False)

            def last_squares(h):
                pe.wait_ge(x3_sq, 2 * KT - 1 + h)
                for c in range(TT // NH):
                    mm = pe.matmul(ps[6 + h][:, c:c + 1], T[:, h, c * P:(c + 1) * P], ones[:, 0:1],
                                   start=False, stop=c == TT // NH - 1)
                mm.then_inc(ssq_ps, 1)

            def ff1(m, c, **hooks):
                unit(U_FF + m, H_FF + 2 * m, Y, more=2 * KT * c, **hooks)

            def behind_first(c, at):
                for m in range(1, KT):
                    ff1(m, c)
                for m in range(KT):
                    unit(U_FF + KT + m, H_FF + 2 * KT + 2 * m, H,
                         (lambda k, h: pe.wait_ge(f_lo, 2 * KT * c + (2 * k + h + 1))) if m == 0 else None,
                         at if m == KT - 1 else {}, 2 * KT * c)

            ff1(0, 0, before=lambda k, h: pe.wait_ge(xg_lo, 2 * k + h + 1),
                at={(0, 1): lambda: column_sums(x2_sum, 2 * KT),
                    (5, 1): lambda: spread(0, 3, 0), (7, 1): lambda: spread(1, 4, 2)})
            with pe.Fori(0, CHUNKS - 1) as c:
                behind_first(c, {})
                ff1(0, c + 1)
            behind_first(CHUNKS - 1, {(3, 1): lambda: (most_squares(0), last_squares(0), most_squares(1)),
                                      (7, 1): lambda: spread(0, 5, 2)})
            last_squares(1)
            spread(1, 6, 0)

        @block.vector
        def _(dve):
            chain = [0]

            def link(ins):
                chain[0] += 1
                ins.then_inc(dve_chain, 1)
                dve.wait_ge(dve_chain, chain[0])

            def factor_columns(n, sums, cols):
                dve.wait_ge(ssq_ps, n + 1)
                dve.tensor_scalar(vcol[:, 1, cols], sums, 1.0 / D, EPS, ALU.mult, ALU.add).then_inc(var_ready, 1)
                dve.wait_ge(var_ready, n + 1)
                dve.wait_ge(std_ready, n + 1)
                inv_newton(cols, rs_col[:, cols])
                link(dve.tensor_copy(rs_hi[:, cols], rs_col[:, cols]))
                link(dve.tensor_tensor(rs_lo[:, cols], rs_col[:, cols], rs_hi[:, cols].bitcast(F32), ALU.subtract))

            def diagonals(h, slot):
                nb = TT // NH
                for part, src in enumerate((rs_hi, rs_lo)):
                    last = dve.tensor_tensor(diag[:, slot + part, :].rearrange("p (c k) -> p c k", c=nb),
                                             ident[:].unsqueeze(1).to_broadcast([P, nb, P]),
                                             src[:, nb * h:nb * (h + 1)].bitcast(F32).unsqueeze(2).to_broadcast([P, nb, P]), ALU.mult)
                last.then_inc(diag_ready, 1)

            def norm_factor(n):
                dve.wait_ge(ident_in, 16)
                factor_columns(n, ps[6][:, 0:TT], slice(0, TT))
                for h in range(NH):
                    diagonals(h, 2 * h)
                for h in range(NH):
                    dve.wait_ge(rsb_ps, 2 * n + h + 1)
                    last = dve.tensor_copy(rs_b[:, hs_(h)], ps[6 + h][:])
                last.then_inc(rsb_set, 1)
                dve.wait_ge(rsb_set, n + 1)

            def inv_newton(cols, res):
                var, root, inv, tmp = (vcol[:, i, cols] for i in range(1, 5))
                link(dve.reciprocal(inv, root))
                link(dve.tensor_tensor(tmp, inv, inv, ALU.mult))
                link(dve.tensor_tensor(tmp, tmp, var, ALU.mult))
                link(dve.tensor_scalar(tmp, tmp, -0.5, 1.5, ALU.mult, ALU.add))
                link(dve.tensor_tensor(res, inv, tmp, ALU.mult))

            def take(hs, dst, more=0):
                dve.wait_ge(half_done, more + (hs + 1))
                h = hs % 2
                return dve.tensor_tensor(dst, bank_of(hs), rs_b[:, hs_(h)], ALU.mult).then_inc(half_free, 1)

            dve.memset(ones[:], 1.0).then_inc(ones_set, 1)
            dve.wait_ge(ones_set, 1)
            dve.tensor_copy(ones_r[:], ones[:, 0:1].to_broadcast([P, P])).then_inc(ones_set, 1)
            dve.memset(rel_sb[BUCKETS:BUCKETS + 1, :], NEG).then_inc(rel_set, 1)
            dve.memset(dw_sb[:], 0.0).then_inc(dw_zero, 1)

            def low_weights(part, hi_done, done):
                dve.wait_ge(hi_done, 1)
                dve.tensor_tensor(WL[:, 0, part], WR[:, 0, part], WH[:, 0, part].bitcast(F32), ALU.subtract).then_inc(done, 1)

            low_weights(w_head, w_head_hi, w_head_split)
            dve.wait_ge(tab_in, 16)
            def sum_sq(k):
                dve.wait_ge(sq_ready, k - 1)
                if k == 2:
                    dve.tensor_copy(sqacc[:], sq[:, 0, :]).then_inc(sq_used, 1)
                else:
                    dve.wait_ge(sq_used, k - 2)
                    dve.tensor_tensor(sqacc[:], sqacc[:], sq[:, k % 2, :], ALU.add).then_inc(sq_used, 1)

            for k in range(KT):
                dve.wait_ge(h_hi, k + 1)
                dve.scalar_tensor_tensor(out=H[:, 1, k, :], in0=xs[:, k, :], scalar=cl[:, C_GMIX + k:C_GMIX + k + 1],
                                         in1=H[:, 0, k, :].bitcast(F32), op0=ALU.mult, op1=ALU.subtract).then_inc(h_lo, 1)
                if k == 0:
                    low_weights(w_body, w_hi_done, w_split)
                if k >= 3:
                    sum_sq(k - 1)
            sum_sq(KT - 1)
            dve.wait_ge(pool_sq, 1)
            dve.wait_ge(sq_used, KT - 2)
            dve.tensor_tensor(sqacc[:], sqacc[:], sqp[:, 0, :], ALU.add).then_inc(sq_used, 1)
            norm_factor(0)
            for hs in range(2 * N_QK):
                take(hs, qk[:, hs // 2, hs_(hs % 2)])
                for g in {3: (0, 1), 7: (2,)}.get(hs, ()):
                    dve.wait_ge(dist_ps, g + 1)
                    dve.tensor_scalar(dist_sb[:, g, :], ps[6 + g % 2][0:HEADS, 0:DIST], DH ** 0.5, None, ALU.mult).then_inc(dist_set, 1)
            def attention(pair):
                jobs = jobs_of(pair)
                base = len(jobs) * pair

                def negated(i):
                    n, (hh, part, t) = base + i, jobs[i]
                    head = 2 * pair + hh
                    W = P * len(key_tiles(part, t))
                    dve.wait_ge(s_ready, n + 1)
                    if n >= 4:
                        dve.wait_ge(t_ready, n - 3)
                    if part == 0:
                        b_ap = bias[:, head, 0, WIDTH - W:WIDTH]
                        o_ap, s_ap = T[:, n % 4, 0:W], ps[S_BANKS[n % 4]][:, 0:W]
                    else:
                        b_ap = bias[:, head, 1:3, WIDTH - W // 2:WIDTH]
                        o_ap, s_ap = (a.rearrange("p (g k) -> p g k", g=2) for a in (T[:, n % 4, 0:W], ps[S_BANKS[n % 4]][:, 0:W]))
                    col = part * 32 + head * TT + t
                    dve.tensor_tensor_reduce(out=o_ap, in0=s_ap, in1=b_ap, scale=-DH ** -0.5, scalar=-NEG, op0=ALU.add,
                                             op1=ALU.min, accum_out=stats[:, col:col + 1]).then_inc(m_ready, 1)

                def main():
                    for i in range(AHEAD, len(jobs) + 5):
                        if i < len(jobs):
                            negated(i)
                        if 0 <= i - 5 < len(jobs):
                            n, (hh, part, t) = base + i - 5, jobs[i - 5]
                            rows = slice(64 * hh, 64 * hh + DH)
                            toks = slice(t * P, (t + 1) * P) if part == 0 else strided(t)
                            dve.wait_ge(pv_done, n + 1)
                            dve.tensor_copy(O[rows, part, pair, toks], ps[n % 2][rows, 0:P]).then_inc(o_free, 1)

                return negated, main

            for t in range(TT):
                last = dve.tensor_tensor_reduce(out=T[:, t // 4, (t % 4) * P:(t % 4 + 1) * P], in0=rs_b[:, strided(t)], in1=ident[:],
                                                scale=1.0, scalar=0.0, op0=ALU.mult, op1=ALU.add, accum_out=rs_col[:, TT + t:TT + t + 1])
            last.then_inc(rs_strided, 1)
            dve.wait_ge(rs_strided, 1)
            dve.wait_ge(dist_out, 48)
            negated, main = attention(0)
            for part in range(2):
                for t in range(1, TT, 2):
                    if part and t == 5:
                        dve.wait_ge(bias_in, 48)
                        negated(0)
                    if part and t == 7:
                        negated(1)
                        negated(2)
                    dve.wait_ge(tmB_done if part else tmA_done, t + 1)
                    dve.tensor_scalar((v12 if part else va0)[:, t, :], ps[t][:], rs_col[:, part * TT + t:part * TT + t + 1], None,
                                      ALU.mult).then_inc(tm_dve, 1)
            negated(3)
            main()

            def gelu2(n, x):
                r = T[:, n % 4, :]
                if len(x.shape) == 3:
                    r = r.rearrange("p (a b) -> p a b", a=x.shape[1])
                dve.wait_ge(g_sq, n + 1)
                link(dve.tensor_scalar(r, r, GELU_A, 1.0, ALU.mult, ALU.add))
                dve.tensor_tensor(r, r, x, ALU.mult).then_inc(g_in, 1)
                dve.wait_ge(g_th, n + 1)
                link(dve.scalar_tensor_tensor(out=x, in0=r, scalar=1.0, in1=x, op0=ALU.add, op1=ALU.mult))

            def gelu_v(n):
                a = 2 * n
                gelu2(n, va0[:, a:a + 2, 0:WIDTH])

            for i in range(4):
                take(H_QK1 + i, qk[:, i // 2, hs_(i % 2)])
                gelu_v(i)
            for t in range(TT):
                link(dve.bn_stats(small[:, t, 0:6], va0[:, t, 0:WIDTH]))
                last = dve.bn_aggr(small[:, t, 6:8], small[:, t, 0:6])
            link(last)
            dve.tensor_scalar(vcol[:, 1, 0:TT], small[:, :, 7], 0.25, EPS, ALU.mult, ALU.add).then_inc(ln_var, 1)
            dve.wait_ge(ln_var, 1)
            dve.wait_ge(ln_std, 1)
            tt = slice(0, TT)
            inv_newton(tt, vcol[:, 0, tt])
            link(dve.tensor_scalar(vcol[:, 0, tt], vcol[:, 0, tt], 0.5, None, ALU.mult))

            def normed(t):
                v = va0[:, t, 0:WIDTH]
                link(dve.tensor_scalar(v, v, small[:, t, 6:7], vcol[:, 0, t:t + 1], ALU.subtract, ALU.mult))
                link(dve.tensor_tensor(v, v, ln_sb[:, 0, :], ALU.mult))
                return dve.tensor_tensor(v, v, ln_sb[:, 1, :], ALU.add)

            dve.wait_ge(mix_in, 16 * MIX_DMAS)
            negated, main = attention(1)
            for i in range(4, 2 * N_QK):
                if i == 2 * N_QK - 1:
                    for ahead in range(AHEAD):
                        negated(ahead)
                take(H_QK1 + i, qk[:, i // 2, hs_(i % 2)])
                last = normed(i - 4)
            last.then_inc(v_ready, 1)
            main()

            def gelu_u(i):
                take(H_MIX + i, u[:, i // 2, hs_(i % 2)])
                dve.wait_ge(half_free, H_MIX + i + 1)
                gelu2(4 + i, u[:, i // 2, hs_(i % 2)])

            gelu_u(0)
            gelu_u(1)
            dve.wait_ge(statsT_ps, 1)
            dve.tensor_copy(rowsT[:], ps[7][:, 0:P]).then_inc(rowsT_set, 1)
            gelu_u(2)
            gelu_u(3)

            def piece(q):
                return q // 2, hs_(q % 2)

            for q in range(4):
                dve.wait_ge(sv_done, q + 1)
                r = T[:, q, :].rearrange("p (c t) -> p c t", c=4)
                dve.tensor_tensor(r, ps[4 + q][:].rearrange("p (c t) -> p c t", c=4),
                                  bs_sb[:, q // 2, :].unsqueeze(1).to_broadcast([P, 4, P]), ALU.add).then_inc(sv_free, 1)
                dve.wait_ge(sv_free, q + 1)
                x = u[:, q // 2, hs_(q % 2)]
                dve.tensor_tensor(x, x, T[:, q, :], ALU.mult).then_inc(y_val[POS_A], 1)

            def doubled(dst, src, back, rows):
                d, s = dst[rows, :], src[rows, :]
                dve.tensor_copy(d[:, 0:back], s[:, 0:back])
                link(dve.tensor_tensor(d[:, back:S], s[:, back:S], s[:, 0:S - back], ALU.add))

            sB, all_rows, lower, upper = sqacc, slice(0, P), slice(0, 64), slice(64, P)

            def pooled(tile):
                doubled(sA, z[:, tile, :], 1, all_rows)
                if tile == 0:
                    doubled(sB, sA, 2, upper)
                else:
                    doubled(sB, sA, 2, all_rows)
                    doubled(sA, sB, 4, all_rows)
                    doubled(sB, sA, 8, upper)
                ratio = cl[:, C_RATIO + 16 * tile:C_RATIO + 16 * (tile + 1)]
                for rows, sums in ((lower, sA), (upper, sB)):
                    s = sums[rows, :]
                    link(dve.tensor_tensor(s[:, 0:16], s[:, 0:16], ratio[rows, :], ALU.mult))
                    last = dve.scalar_tensor_tensor(out=z[rows, tile, :], in0=s, scalar=cl[rows, C_WINV + tile:C_WINV + tile + 1],
                                                    in1=z[rows, tile, :], op0=ALU.mult, op1=ALU.subtract)
                return last

            take(H_MIX + 4, zz(0))
            take(H_MIX + 5, zz(1))
            dve.wait_ge(half_free, H_MIX + 6)
            link(pooled(0))

            dve.wait_ge(rows_in, 16)
            nat = lambda a: a.rearrange("h (p r) -> h p r", r=4)
            per = lambda a: a.rearrange("h (r p) -> h p r", r=4)
            neg0, neg1, den0, den1 = nat(R[:, 0, :]), per(R[:, 1, :]), nat(R[:, 2, :]), per(R[:, 3, :])
            e0, e1, t0, t1, inv = nat(R[:, 0, :]), nat(rt[:, 1, :]), nat(rt[:, 0, :]), nat(R[:, 1, :]), nat(R[:, 2, :])
            link(dve.tensor_tensor(t0, neg0, neg1, ALU.min))
            link(dve.tensor_tensor(e1, t0, neg1, ALU.subtract))
            dve.tensor_tensor(e0, t0, neg0, ALU.subtract).then_inc(rexp_in, 1)
            dve.wait_ge(rexp_out, 2)
            dve.tensor_tensor(t0, e0, den0, ALU.mult)
            link(dve.tensor_tensor(t1, e1, den1, ALU.mult))
            link(dve.tensor_tensor(t0, t0, t1, ALU.add))
            link(dve.reciprocal(R[:, 2, :], rt[:, 0, :]))
            dve.tensor_tensor(e0, e0, inv, ALU.mult)
            dve.tensor_tensor(e1, e1, inv, ALU.mult).then_inc(mixw_set, 1)

            take(H_MIX + 6, zz(2))
            take(H_MIX + 7, zz(3))
            dve.wait_ge(half_free, H_MIX + 8)
            pooled(1).then_inc(pool_ready, 1)

            for i in range(8, 12):
                take(H_MIX + i, tc[:, (i - 8) // 2, hs_(i % 2)])

            def low(pos, n, val, dst, scale=1.0):
                dve.wait_ge(y_hi[pos], n + 1)
                dve.scalar_tensor_tensor(out=Y[:, 1, 2 * pos + dst[0], dst[1]], in0=val, scalar=scale,
                                         in1=Y[:, 0, 2 * pos + dst[0], dst[1]].bitcast(F32),
                                         op0=ALU.mult, op1=ALU.subtract).then_inc(y_lo[pos], 1)

            def attn_mix(pr):
                a, b = O[:, 0, pr, :], O[:, 1, pr, :]
                dve.tensor_tensor(a, a, wb[:, 0, pr, :], ALU.mult)
                link(dve.tensor_tensor(b, b, wb[:, 1, pr, :], ALU.mult))
                dve.tensor_tensor(a, a, b, ALU.add).then_inc(y_val[POS_C], 1)

            def conv(tile):
                c, x = cv[:, tile, :], tc[:, tile, :]
                w = [cl[:, C_CONV + 2 * j + tile:C_CONV + 2 * j + tile + 1] for j in range(3)]
                link(dve.tensor_scalar(c, x, w[2], None, ALU.mult))
                for back in (1, 2):
                    link(dve.scalar_tensor_tensor(out=c[:, back:S], in0=x[:, 0:S - back], scalar=w[2 - back],
                                                  in1=c[:, back:S], op0=ALU.mult, op1=ALU.add))

            def conv_in(i):
                take(H_MIX + i, T[:, i % 4, :])
                dve.wait_ge(half_free, H_MIX + i + 1)
                x = tc[:, (i - 12) // 2, hs_(i % 2)]
                return dve.tensor_tensor(x, x, T[:, i % 4, :], ALU.mult)

            dve.wait_ge(wb_in, 16 * 8)
            attn_mix(0)
            attn_mix(1)
            dve.wait_ge(y_val[POS_C], 2)
            for tile in range(BT):
                conv_in(12 + 2 * tile)
                link(conv_in(13 + 2 * tile))
                conv(tile)
            for q in range(4):
                low(POS_A, q, u[:, q // 2, hs_(q % 2)], piece(q), 0.5)
            dve.wait_ge(dmm_done, 4)
            for q in range(4):
                low(POS_D, q, ps[4 + q][:], piece(q), cl[:, C_DSC + q // 2:C_DSC + q // 2 + 1])
            for pr in range(BT):
                low(POS_C, pr, O[:, 0, pr, :], (pr, slice(0, S)))
            for q in range(5):
                if q < 4:
                    take(H_MIX + 16 + q, T[:, q, :])
                    dve.wait_ge(half_free, H_MIX + 16 + q + 1)
                    x = cv[:, q // 2, hs_(q % 2)]
                    dve.tensor_tensor(x, x, T[:, q, :], ALU.mult).then_inc(y_val[POS_B], 1)
                if q >= 1:
                    low(POS_B, q - 1, cv[:, (q - 1) // 2, hs_((q - 1) % 2)], piece(q - 1))

            def gate_take(n, j=0):
                take(H_GATE + n, T[:, n % 4, :], 8 * j)

            def gate_terms(n, j):
                b, h = n // 2, n % 2
                dve.wait_ge(tanh_done, 8 * j + (n + 1))
                dve.wait_ge(y_ps, 8 * j + (n + 1))
                r, m = T[:, n % 4, :], M[:, j, hs_(h)]
                ins = dve.scalar_tensor_tensor(out=m if b == 0 else r, in0=r, scalar=1.0, in1=ps[4 + n % 2][:],
                                               op0=ALU.add, op1=ALU.mult).then_inc(y_free, 1)
                if b:
                    dve.wait_ge(y_free, 8 * j + (n + 1))
                    ins = dve.tensor_tensor(m, m, r, ALU.add)
                if b == 3:
                    ins.then_inc(m_set, 1)

            gate_take(0)
            with dve.Fori(0, KT - 1) as j:
                for n in range(8):
                    gate_take(n + 1, j)
                    gate_terms(n, j)
            for n in range(6):
                gate_take(n + 1, KT - 1)
                gate_terms(n, KT - 1)
            gate_take(7, KT - 1)
            for i, (h, k) in enumerate(DVE_LOWS):
                if i == 2:
                    gate_terms(6, KT - 1)
                if i == 3:
                    gate_terms(7, KT - 1)
                dve.wait_ge(m_hi, KT * h + k + 1)
                dve.tensor_tensor(H[:, 1, k, hs_(h)], M[:, k, hs_(h)], H[:, 0, k, hs_(h)].bitcast(F32), ALU.subtract).then_inc(m_lo, 1)

            def acc_sq(n, ready, done):
                dve.wait_ge(ready, n + 1)
                a = sqacc[:, hs_(n % 2)]
                if n < 2:
                    dve.tensor_copy(a, T[:, n % 2, :]).then_inc(done, 1)
                else:
                    dve.wait_ge(done, n - 1)
                    dve.tensor_tensor(a, a, T[:, n % 2, :], ALU.add).then_inc(done, 1)

            for n in range(2 * KT + 1):
                if n < 2 * KT:
                    j, h = n // 2, n % 2
                    dve.wait_ge(xr_in[n % 2], 16 * (n // 2 + 1))
                    dve.wait_ge(half_done, H_WO + n + 1)
                    dve.scalar_tensor_tensor(out=M[:, j, hs_(h)], in0=bank_of(H_WO + n), scalar=0.5, in1=T[:, 2 + n % 2, :],
                                             op0=ALU.mult, op1=ALU.add).then_inc(half_free, 1)
                if n >= 1:
                    j, h = (n - 1) // 2, (n - 1) % 2
                    dve.wait_ge(xg_hi, n)
                    dve.scalar_tensor_tensor(out=Y[:, 1, j, hs_(h)], in0=M[:, j, hs_(h)], scalar=cl[:, C_GFF + j:C_GFF + j + 1],
                                             in1=Y[:, 0, j, hs_(h)].bitcast(F32), op0=ALU.mult, op1=ALU.subtract).then_inc(xg_lo, 1)
                    acc_sq(n - 1, x2_sq, x2_sum)
            norm_factor(1)

            def final_scale(h, tiles):
                dve.wait_ge(rsb_set, 3 + h)
                for m in tiles:
                    dve.wait_ge(x3_g, 2 * m + h + 1)
                    dve.tensor_tensor(M[:, m, hs_(h)], M[:, m, hs_(h)], rs_b[:, hs_(h)], ALU.mult).then_inc(out_dve, 1)

            def hidden(c):
                for n in range(2 * KT + 1):
                    if n < 2 * KT:
                        dve.wait_ge(half_done, 4 * KT * c + (H_FF + n + 1))
                        dve.scalar_tensor_tensor(out=T[:, n % 4, :], in0=bank_of(H_FF + n), scalar=0.0, in1=rs_b[:, hs_(n % 2)],
                                                 op0=ALU.max, op1=ALU.mult).then_inc(half_free, 1)
                    if n >= 1:
                        m, h = (n - 1) // 2, (n - 1) % 2
                        dve.wait_ge(f_hi, 2 * KT * c + n)
                        dve.tensor_tensor(H[:, 1, m, hs_(h)], T[:, (n - 1) % 4, :], H[:, 0, m, hs_(h)].bitcast(F32),
                                          ALU.subtract).then_inc(f_lo, 1)

            def add_chunk(n, c):
                m = M[:, n // 2, hs_(n % 2)]
                dve.wait_ge(half_done, 4 * KT * c + (H_FF + 2 * KT + n + 1))
                dve.tensor_tensor(m, m, bank_of(H_FF + 2 * KT + n), ALU.add).then_inc(half_free, 1)

            with dve.Fori(0, CHUNKS - 1) as c:
                hidden(c)
                for n in range(2 * KT):
                    add_chunk(n, c)
            hidden(CHUNKS - 1)
            for n in range(2 * KT):
                add_chunk(n, CHUNKS - 1)
                if 1 <= n <= 2 * KT - 2:
                    acc_sq(n - 1, x3_sq, x3_sum)
                if n == 2 * KT - 2:
                    factor_columns(2, ps[6][:, 0:4], slice(0, 4))
                    diagonals(0, 2)
            final_scale(0, OUT_DVE[0][:1])
            final_scale(0, OUT_DVE[0][1:2])
            factor_columns(3, ps[7][:, 0:4], slice(4, 8))
            diagonals(1, 0)
            final_scale(0, OUT_DVE[0][2:])
            final_scale(1, OUT_DVE[1])

        @block.scalar
        def _(act):
            def root(n, cols, ready, done):
                act.wait_ge(ready, n + 1)
                act.activation(vcol[:, 2, cols], vcol[:, 1, cols], ACT.Sqrt).then_inc(done, 1)

            act.wait_ge(ones_set, 1)
            act.activation(vcol[:, 4, 0:1], ones[:, 0:1], ACT.Sqrt)
            act.wait_ge(w_head_in, 16)
            act.activation(WH[:, 0, w_head], WR[:, 0, w_head], ACT.Copy).then_inc(w_head_hi, 1)
            act.wait_ge(tab_in, 16)
            for k in range(KT):
                act.wait_ge(x_in[k], 16)
                act.activation(H[:, 0, k, :], xs[:, k, :], ACT.Copy, scale=cl[:, C_GMIX + k:C_GMIX + k + 1]).then_inc(h_hi, 1)
                if k == 0:
                    act.wait_ge(w_in[0], 16)
                    act.activation(WH[:, 0, w_body], WR[:, 0, w_body], ACT.Copy).then_inc(w_hi_done, 1)
                if k >= 2:
                    if k >= 4:
                        act.wait_ge(sq_used, k - 3)
                    act.activation(sq[:, k % 2, :], xs[:, k, :], ACT.Square).then_inc(sq_ready, 1)
            root(0, slice(0, TT), var_ready, std_ready)
            act.wait_ge(dist_set, 3)
            for g in range(3):
                act.dma_start(dist_dram[g], dist_sb[:, g, :].unsqueeze(1).to_broadcast([HEADS, P, DIST])).then_inc(dist_out, 16)
            act.wait_ge(dist_out, 48)
            for t in range(0, TT, 2):
                act.wait_ge(tmA_done, t + 1)
                act.wait_ge(rsb_set, 1)
                act.activation(va0[:, t, :], ps[t][:], ACT.Copy, scale=rs_col[:, t:t + 1]).then_inc(tm_act, 1)
            for g in range(3):
                toeplitz = dist_dram[g].rearrange("h p d -> h (p d)")[:, P - 1:P - 1 + P * (DIST - 1)]
                toeplitz = toeplitz.rearrange("h (p d) -> p h d", d=DIST - 1)[:, :, 0:WIDTH]
                act.dma_start(bias[:, :, g, :], toeplitz).then_inc(bias_in, 16)
            act.wait_ge(rs_strided, 1)
            for t in range(0, TT, 2):
                act.wait_ge(tmB_done, t + 1)
                act.activation(v12[:, t, :], ps[t][:], ACT.Copy, scale=rs_col[:, TT + t:TT + t + 1]).then_inc(tm_act, 1)

            def attention(pair):
                jobs = jobs_of(pair)
                base = len(jobs) * pair
                for i in range(len(jobs) + 3):
                    if 0 <= i - 1 < len(jobs):
                        n, (hh, part, t) = base + i - 1, jobs[i - 1]
                        W = P * len(key_tiles(part, t))
                        col = part * 32 + (2 * pair + hh) * TT + t
                        act.wait_ge(m_ready, n + 1)
                        act.activation(T[:, n % 4, 0:W], T[:, n % 4, 0:W], ACT.Exp, scale=-1.0, bias=stats[:, col:col + 1],
                                       accum_out=stats[:, 64 + col:65 + col]).then_inc(p_ready, 1)
                    if 0 <= i - 3 < len(jobs):
                        n, (hh, part, t) = base + i - 3, jobs[i - 3]
                        W = P * len(key_tiles(part, t))
                        act.wait_ge(t_ready, n + 1)
                        if n >= 2:
                            act.wait_ge(pv_done, n - 1)
                        act.activation(pts[:, n % 2, 0:W], ps[6 + n % 2][:, 0:W], ACT.Copy).then_inc(t_free, 1)

            attention(0)

            def gelu2(n, x):
                r = T[:, n % 4, :]
                if len(x.shape) == 3:
                    r = r.rearrange("p (a b) -> p a b", a=x.shape[1])
                act.activation(r, x, ACT.Square).then_inc(g_sq, 1)
                act.wait_ge(g_in, n + 1)
                act.activation(r, r, ACT.Tanh, scale=GELU_B).then_inc(g_th, 1)

            for n in range(4):
                gelu2(n, va0[:, 2 * n:2 * n + 2, 0:WIDTH])
            root(0, slice(0, TT), ln_var, ln_std)
            attention(1)

            def gelu_u(i):
                act.wait_ge(half_free, H_MIX + i + 1)
                gelu2(4 + i, u[:, i // 2, hs_(i % 2)])

            gelu_u(0)
            gelu_u(1)
            act.wait_ge(rowsT_set, 1)
            act.dma_start(stat_dram, rowsT[:]).then_inc(stat_out, 16)
            gelu_u(2)
            gelu_u(3)
            act.wait_ge(stat_out, 16)
            act.dma_start(R[:], stat_dram.rearrange("(s hb t) q -> hb s (t q)", s=4, hb=8)).then_inc(rows_in, 16)
            act.wait_ge(rexp_in, 1)
            for e in (R[:, 0, :], rt[:, 1, :]):
                act.activation(e, e, ACT.Exp).then_inc(rexp_out, 1)
            act.wait_ge(mixw_set, 1)
            for part, e in enumerate((R[:, 0, :], rt[:, 1, :])):
                act.dma_start(mixw_dram[part].rearrange("h (b t) -> (h b) t", b=2), e).then_inc(mixw_out, 16)
            act.wait_ge(mixw_out, 32)
            for part in range(2):
                for head in range(HEADS):
                    rows = slice(64 * (head % 2), 64 * (head % 2) + 64)
                    act.dma_start(wb[rows, part, head // 2, :], mixw_dram[part, head].partition_broadcast(64)).then_inc(wb_in, 16)

            def high(pos, n, ready, val, dst, scale=1.0):
                act.wait_ge(ready, n + 1)
                act.activation(Y[:, 0, 2 * pos + dst[0], dst[1]], val, ACT.Copy, scale=scale).then_inc(y_hi[pos], 1)

            act.wait_ge(pool_ready, 1)
            for q in range(4):
                high(POS_A, q, y_val[POS_A], u[:, q // 2, hs_(q % 2)], (q // 2, hs_(q % 2)), 0.5)
            act.wait_ge(y_val[POS_C], 2)
            for pr in range(BT):
                high(POS_C, pr, y_val[POS_C], O[:, 0, pr, :], (pr, slice(0, S)))
            for q in range(4):
                high(POS_D, q, dmm_done, ps[4 + q][:], (q // 2, hs_(q % 2)), cl[:, C_DSC + q // 2:C_DSC + q // 2 + 1])
            for q in range(4):
                high(POS_B, q, y_val[POS_B], cv[:, q // 2, hs_(q % 2)], (q // 2, hs_(q % 2)))

            def gate_tanh(n, j):
                act.wait_ge(half_free, 8 * j + (H_GATE + n + 1))
                act.activation(T[:, n % 4, :], T[:, n % 4, :], ACT.Tanh, scale=0.5).then_inc(tanh_done, 1)

            with act.Fori(0, KT - 1) as j:
                for n in range(8):
                    gate_tanh(n, j)
            for n in range(7):
                gate_tanh(n, KT - 1)

            def reload_x(n):
                if n >= 2:
                    act.wait_ge(half_free, H_WO + n - 1)
                act.dma_start(T[:, 2 + n % 2, :], xT[(n // 2) * P:(n // 2 + 1) * P, hs_(n % 2)]).then_inc(xr_in[n % 2], 16)

            act.wait_ge(half_done, H_WO)
            act.wait_ge(m_set, 2 * KT - 2)
            for n in range(2 * KT):
                h, k = divmod(n, KT)
                if n == 2:
                    gate_tanh(7, KT - 1)
                if n == KT - 1:
                    act.wait_ge(m_set, 2 * KT - 1)
                if n == KT:
                    act.wait_ge(m_set, 2 * KT)
                    reload_x(0)
                    reload_x(1)
                act.activation(H[:, 0, k, hs_(h)], M[:, k, hs_(h)], ACT.Copy).then_inc(m_hi, 1)
            for n in range(2 * KT):
                j, h = n // 2, n % 2
                act.wait_ge(half_free, H_WO + n + 1)
                act.activation(Y[:, 0, j, hs_(h)], M[:, j, hs_(h)], ACT.Copy, scale=cl[:, C_GFF + j:C_GFF + j + 1]).then_inc(xg_hi, 1)
                if n >= 2:
                    act.wait_ge(x2_sum, n - 1)
                act.activation(T[:, n % 2, :], M[:, j, hs_(h)], ACT.Square).then_inc(x2_sq, 1)
                if n + 2 < 2 * KT:
                    reload_x(n + 2)
            root(1, slice(0, TT), var_ready, std_ready)

            with act.Fori(0, CHUNKS) as c:
                for n in range(2 * KT):
                    act.wait_ge(half_free, 4 * KT * c + (H_FF + n + 1))
                    r = T[:, n % 4, :]
                    act.activation(r, r, ACT.Square).then_inc(f_sq, 1)
                    act.wait_ge(f_sq, 2 * KT * c + (n + 1))
                    act.activation(H[:, 0, n // 2, hs_(n % 2)], r, ACT.Copy).then_inc(f_hi, 1)

            def final_factor(h):
                root(2 + h, slice(4 * h, 4 * h + 4), var_ready, std_ready)
                act.wait_ge(rsb_ps, 5 + h)
                act.activation(rs_b[:, hs_(h)], ps[6 + h][:], ACT.Copy).then_inc(rsb_set, 1)

            for n in range(2 * KT):
                m = M[:, n // 2, hs_(n % 2)]
                act.wait_ge(half_free, H_FF + 4 * KT * (CHUNKS - 1) + 2 * KT + n + 1)
                if n >= 2:
                    act.wait_ge(x3_sum, n - 1)
                act.activation(T[:, n % 2, :], m, ACT.Square).then_inc(x3_sq, 1)
                act.activation(m, m, ACT.Copy, scale=cl[:, C_GFIN + n // 2:C_GFIN + n // 2 + 1]).then_inc(x3_g, 1)
                if n == 2 * KT - 2:
                    final_factor(0)
            final_factor(1)
            for i, m in enumerate(OUT_POOL[1]):
                act.wait_ge(out_pool, len(OUT_POOL[0]) + i + 1)
                act.dma_start(out[m * P:(m + 1) * P, hs_(1)], M[:, m, hs_(1)]).then_inc(out_sent, 16)


def key_tiles(part, t):
    if part == 0:
        return [(0, k) for k in range(max(t - 1, 0), t + 1)]
    blk, r = divmod(t, 4)
    return [(g, 4 * b + r) for g in range(2) for b in range(blk + 1)]


def t5_bucket(dist):
    exact = BUCKETS // 2
    d = np.maximum(dist, 1).astype(np.float32)
    large = exact + (np.log(d / np.float32(exact)) / np.float32(np.log(2048 / exact)) * (BUCKETS - exact)).astype(np.int32)
    return np.where(dist < exact, dist, np.minimum(large, BUCKETS - 1))


def distance_onehot():
    e = np.zeros((BUCKETS + 1, 3, DIST), np.float32)
    for g, dil in enumerate((1, 4, 16)):
        for i in range(DIST):
            diff = 255 - i
            step = 4 if g == 2 else 1
            ok = 0 <= diff <= P * step and diff % step == 0
            row = int(t5_bucket(np.array(diff // step * dil))) if ok else BUCKETS
            e[row, g, i] = 1.0
    return e


def kernel(**inputs):
    import concourse.bacc as bacc
    from concourse.bass_utils import run_bass_kernel_spmd as run

    a = {k: np.asarray(v) for k, v in inputs.items()}
    w_in = a["w_in"][0]
    cuts = np.cumsum([0, WIDTH, WIDTH, WIDTH, WIDTH, WIDTH, 768, 768, 768, WIDTH])
    A_U, A_V, B_B, B_C, B_X, C_Q, C_K, C_V, D_Z, GATES = (int(x) for x in cuts)

    def block(w, c):
        return w[:, c:c + P].reshape(-1, P, P).transpose(1, 0, 2).reshape(P, -1)

    units = []
    for pair in range(2):
        qk = [block(w_in, base + g * WIDTH + pair * P) for g in range(3) for base in (C_Q, C_K)]
        units += qk
        if pair == 0:
            for wide in (np.concatenate([w_in[:, A_V:A_V + WIDTH], w_in[:, C_V:C_V + WIDTH]], 1),
                         w_in[:, C_V + WIDTH:C_V + 3 * WIDTH]):
                units += [w.transpose(1, 0, 2).reshape(P, UNIT) for w in wide.reshape(4, 2, P, HALF)]
    units += [block(w_in, base + m * P) for base in (A_U, D_Z, B_C, B_X, B_B) for m in range(BT)]
    w1 = np.stack(units)
    outs = {POS_A: a["w_a_out"][0], POS_B: a["w_b_out"][0], POS_C: a["w_c_out"][0], POS_D: a["w_d_out"][0]}
    w2 = np.stack([np.concatenate([block(w_in, GATES + REF_GATE[pos] * D + j * P), block(outs[pos], j * P)], 1)
                   for j in range(KT) for pos in GATE_ORDER])
    f1, f2 = a["w_ff1"][0], a["w_ff2"][0]
    units = [block(a["w_o"][0], j * P) for j in range(KT)]
    for c in range(CHUNKS):
        units += [block(f1, c * D + m * P) for m in range(KT)]
        units += [block(f2[c * D:(c + 1) * D], m * P) for m in range(KT)]
    w3 = np.stack(units)

    cols = np.zeros((P, N_COLS), np.float32)
    cols[:, C_GMIX:C_GMIX + KT] = a["norm_mix_g"][0].reshape(KT, P).T
    cols[:, C_GFF:C_GFF + KT] = a["norm_ff_g"][0].reshape(KT, P).T
    cols[:, C_GFIN:C_GFIN + KT] = a["final_g"].reshape(KT, P).T
    cols[:, C_CONV:C_CONV + 6] = a["b_conv"][0].reshape(3 * BT, P).T
    cols[:, C_DSC:C_DSC + BT] = a["d_scale"][0].reshape(BT, P).T
    windows = np.repeat(np.array([2, 4, 8, 16], np.float32), 64).reshape(BT, P)
    cols[:, C_WINV:C_WINV + BT] = (1 / windows).T
    t = np.arange(1, 17, dtype=np.float32)
    cols[:, C_RATIO:] = (windows[:, :, None] / np.minimum(t, windows[:, :, None])).transpose(1, 0, 2).reshape(P, -1)

    arrays = {
        "xT": np.ascontiguousarray(a["x"][0].T), "cols": cols, "eye": np.eye(P, dtype=np.float32),
        "onehot": distance_onehot(), "rel": a["rel_bias"],
        "lnrow": np.stack([a["a_ln_g"][0], a["a_ln_b"][0]]), "bsrow": a["a_bs"][0],
        "wsT": np.ascontiguousarray(a["a_ws"][0].transpose(2, 0, 1)), "dw": a["d_w"][0],
        "w1": w1, "w2": w2, "w3": w3,
    }
    nc = bacc.Bacc("TRN2", target_bir_lowering=False, num_devices=1)
    aps = [nc.dram_tensor(f"in_{n}", v.shape, mybir.dt.from_np(v.dtype), kind="ExternalInput").ap() for n, v in arrays.items()]
    outT = nc.dram_tensor("outT", (D, S), F32, kind="ExternalOutput").ap()
    build(nc, *aps, outT)
    r = run(nc, [{f"in_{n}": v for n, v in arrays.items()}], core_ids=[0])
    return r.results[0]["outT"].T.reshape(1, S, D)
```
